# Optimizing a Trainium2 kernel written in Bass

```python
import jax
import jax.numpy as jnp
from jax import lax
import numpy as np
import math
import jax, jax.numpy as jnp

D_MODEL = 1024
BATCH = 1
SEQ = 512
DEPTH = 1

EPS = 1e-6
HG_HEADS = 8
HG_DK = 128
HG_DV = D_MODEL // HG_HEADS
HG_KW = HG_HEADS * HG_DK
HG_VW = HG_HEADS * HG_DV
HG_CHUNK = 32
CONV_WIDTH = D_MODEL
CONV_K = 31
IN_SIZES = (HG_KW, HG_KW, HG_VW, HG_VW, CONV_WIDTH, CONV_WIDTH, D_MODEL, D_MODEL)
IN_SPLITS = tuple(int(s) for s in np.cumsum(IN_SIZES)[:-1])
N_IN = sum(IN_SIZES)
PEER_HEADS = 8
PEER_NKEYS = 128
PEER_EXPERTS = PEER_NKEYS * PEER_NKEYS
PEER_DQ = 256
PEER_TOPK = 16
PEER_BLOCK = 128


def rms_norm(x, g):
    xf = x.astype(jnp.float32)
    y = xf * lax.rsqrt(jnp.mean(xf * xf, axis=-1, keepdims=True) + EPS)
    return (y * g.astype(jnp.float32)).astype(x.dtype)

def layer_norm(x, g, b):
    xf = x.astype(jnp.float32)
    mu = jnp.mean(xf, axis=-1, keepdims=True)
    xc = xf - mu
    y = xc * lax.rsqrt(jnp.mean(xc * xc, axis=-1, keepdims=True) + EPS)
    return (y * g.astype(jnp.float32) + b.astype(jnp.float32)).astype(x.dtype)

def hgrn2_chunkwise(q, k, v, logf):
    B, S, H, dk = q.shape
    dv = v.shape[-1]
    n = S // HG_CHUNK

    def to_chunks(t):
        return t.reshape(B, n, HG_CHUNK, H, t.shape[-1]).transpose(1, 0, 3, 2, 4)

    causal = jnp.tril(jnp.ones((HG_CHUNK, HG_CHUNK), dtype=bool))

    def step(state, inp):
        qt, kt, vt, lt = inp
        bcum = jnp.cumsum(lt, axis=2)
        rel = bcum[:, :, :, None, :] - bcum[:, :, None, :, :]
        decay = jnp.exp(jnp.where(causal[:, :, None], rel, -jnp.inf))
        scores = jnp.einsum('bhtk,bhsk,bhtsk->bhts', qt, kt, decay)
        o = jnp.einsum('bhts,bhsv->bhtv', scores, vt)
        o = o + jnp.einsum('bhtk,bhkv->bhtv', qt * jnp.exp(bcum), state)
        blast = bcum[:, :, -1:, :]
        state = (jnp.exp(blast[:, :, 0, :])[..., None] * state
                 + jnp.einsum('bhsk,bhsv->bhkv', kt * jnp.exp(blast - bcum), vt))
        return state, o

    s0 = jnp.zeros((B, H, dk, dv), jnp.float32)
    _, o = lax.scan(step, s0, (to_chunks(q), to_chunks(k), to_chunks(v), to_chunks(logf)))
    return o.transpose(1, 0, 3, 2, 4).reshape(B, S, H, dv)

def causal_depthwise_conv(u, w, b):
    y = lax.conv_general_dilated(
        u, w[:, None, :].astype(u.dtype), window_strides=(1,),
        padding=((CONV_K - 1, 0),), dimension_numbers=('NWC', 'WIO', 'NWC'),
        feature_group_count=u.shape[-1])
    return y + b

def peer_layer(h, w_q, sub_keys, u_tab, v_tab):
    B, S, D = h.shape
    T = B * S
    hf = h.reshape(T, D)
    q = (hf @ w_q).reshape(T, PEER_HEADS, 2, PEER_DQ // 2)
    s = jnp.einsum('thpd,hpnd->thpn', q, sub_keys)
    sc, idx = lax.top_k(s, PEER_TOPK)
    cand = (sc[:, :, 0, :, None] + sc[:, :, 1, None, :]).reshape(T, PEER_HEADS, PEER_TOPK * PEER_TOPK)
    cidx = (idx[:, :, 0, :, None] * PEER_NKEYS + idx[:, :, 1, None, :]).reshape(T, PEER_HEADS, PEER_TOPK * PEER_TOPK)
    top_sc, pos = lax.top_k(cand, PEER_TOPK)
    eidx = jnp.take_along_axis(cidx, pos, axis=-1)
    gate = jax.nn.softmax(top_sc.astype(jnp.float32), axis=-1).astype(h.dtype)
    nb = T // PEER_BLOCK

    def block(args):
        hb, eb, gb = args
        act = jax.nn.gelu(jnp.einsum('thkd,td->thk', u_tab[eb], hb), approximate=False)
        return jnp.einsum('thk,thkd->td', gb * act, v_tab[eb])

    y = lax.map(block, (hf.reshape(nb, PEER_BLOCK, D),
                        eidx.reshape(nb, PEER_BLOCK, PEER_HEADS, PEER_TOPK),
                        gate.reshape(nb, PEER_BLOCK, PEER_HEADS, PEER_TOPK)))
    return y.reshape(B, S, D)

def first_inputs(seed: int = 0) -> dict:
    key = jax.random.key(seed)
    ks = jax.random.split(key, 24)
    L = DEPTH

    def nrm(k, shape, scale):
        return jax.random.normal(k, shape, jnp.float32) * scale

    return {
        'x': nrm(ks[0], (BATCH, SEQ, D_MODEL), 1.0),
        'c': nrm(ks[1], (BATCH, D_MODEL), 1.0),
        'ada_w': nrm(ks[2], (L, D_MODEL, 6 * D_MODEL), 0.5 * D_MODEL ** -0.5),
        'ada_b': nrm(ks[3], (L, 6 * D_MODEL), 0.02),
        'norm1_g': 1.0 + nrm(ks[4], (L, D_MODEL), 0.02),
        'w_in': nrm(ks[5], (L, D_MODEL, N_IN), D_MODEL ** -0.5),
        'lb_logits': nrm(ks[6], (L + 1, HG_KW), 0.5),
        'hg_norm_g': 1.0 + nrm(ks[7], (L, HG_VW), 0.02),
        'w_a': nrm(ks[8], (L, HG_VW, D_MODEL), HG_VW ** -0.5),
        'conv_w': nrm(ks[9], (L, CONV_K, CONV_WIDTH), CONV_K ** -0.5),
        'conv_b': nrm(ks[10], (L, CONV_WIDTH), 0.02),
        'conv_ln_g': 1.0 + nrm(ks[11], (L, CONV_WIDTH), 0.02),
        'conv_ln_b': nrm(ks[12], (L, CONV_WIDTH), 0.02),
        'w_b': nrm(ks[13], (L, CONV_WIDTH, D_MODEL), CONV_WIDTH ** -0.5),
        'w_out': nrm(ks[14], (L, D_MODEL, D_MODEL), D_MODEL ** -0.5),
        'norm2_g': 1.0 + nrm(ks[15], (L, D_MODEL), 0.02),
        'peer_wq': nrm(ks[16], (L, D_MODEL, PEER_HEADS * PEER_DQ), D_MODEL ** -0.5),
        'peer_keys': nrm(ks[17], (L, PEER_HEADS, 2, PEER_NKEYS, PEER_DQ // 2), (PEER_DQ // 2) ** -0.5),
        'peer_u': nrm(ks[18], (L, PEER_EXPERTS, D_MODEL), D_MODEL ** -0.5),
        'peer_v': nrm(ks[19], (L, PEER_EXPERTS, D_MODEL), PEER_HEADS ** -0.5),
        'final_g': 1.0 + nrm(ks[20], (D_MODEL,), 0.02),
    }

def first_block(x, c, ada_w, ada_b, norm1_g, w_in, lb_logits, hg_norm_g, w_a, conv_w, conv_b,
              conv_ln_g, conv_ln_b, w_b, w_out, norm2_g, peer_wq, peer_keys, peer_u, peer_v,
              final_g):
    B, S, D = x.shape
    lower_bounds = jnp.cumsum(jax.nn.softmax(lb_logits.astype(jnp.float32), axis=0), axis=0)

    def heads(t):
        return t.reshape(B, S, HG_HEADS, -1)

    h = x
    for l in range(DEPTH):
        ada = (jax.nn.silu(c) @ ada_w[l] + ada_b[l])[:, None, :]
        sh1, sc1, g1, sh2, sc2, g2 = jnp.split(ada, 6, axis=-1)

        u = rms_norm(h, norm1_g[l]) * (1 + sc1) + sh1
        z = u @ w_in[l]
        zq, zf, zi, zg, zca, zcb, zga, zgb = jnp.split(z, IN_SPLITS, axis=-1)

        lb = lower_bounds[l]
        f = lb + (1.0 - lb) * jax.nn.sigmoid(zf.astype(jnp.float32))
        o = hgrn2_chunkwise(heads(zq.astype(jnp.float32)), heads(1.0 - f),
                            heads(zi.astype(jnp.float32)), heads(jnp.log(f)))
        o = rms_norm(o, hg_norm_g[l].reshape(HG_HEADS, HG_DV)).reshape(B, S, HG_VW).astype(x.dtype)
        y_a = (o * jax.nn.silu(zg)) @ w_a[l]

        glu = zca * jax.nn.sigmoid(zcb)
        cv = causal_depthwise_conv(glu, conv_w[l], conv_b[l])
        cv = jax.nn.silu(layer_norm(cv, conv_ln_g[l], conv_ln_b[l]))
        y_b = cv @ w_b[l]

        merged = jax.nn.sigmoid(zga) * y_a + jax.nn.sigmoid(zgb) * y_b
        h = h + g1 * (merged @ w_out[l])

        u2 = rms_norm(h, norm2_g[l]) * (1 + sc2) + sh2
        h = h + g2 * peer_layer(u2, peer_wq[l], peer_keys[l], peer_u[l], peer_v[l])

    return rms_norm(h, final_g)


DEPTH_2 = 2

N_MIXERS = 3
HEAD_DIM = 64
BLOCK = 128
D_FF = 4 * D_MODEL

A_HEADS = D_MODEL // HEAD_DIM
A_GROUPS = ((128, 1, 6), (512, 4, 5), (2048, 16, 5))
B_HEADS = D_MODEL // (2 * HEAD_DIM)
C_HEADS = D_MODEL // HEAD_DIM
C_KV_HEADS = 4
C_GROUP = C_HEADS // C_KV_HEADS
GRID_W = 64
ROPE_THETA = 10000.0
AXIS_ROPE_DIM = HEAD_DIM // 2
NUM_BUCKETS = 32
REL_MAX_DISTANCE = 1024
REL_BIAS_HEADS = A_HEADS


def rms_norm_2(x, g):
    xf = x.astype(jnp.float32)
    y = xf * lax.rsqrt(jnp.mean(xf * xf, axis=-1, keepdims=True) + EPS)
    return (y * g.astype(jnp.float32)).astype(x.dtype)

def t5_bucket(rel):
    nb = NUM_BUCKETS // 2
    max_exact = nb // 2
    side = jnp.where(rel > 0, nb, 0)
    n = jnp.abs(rel)
    nf = jnp.maximum(n, 1).astype(jnp.float32)
    large = max_exact + (jnp.log(nf / max_exact) / math.log(REL_MAX_DISTANCE / max_exact)
                         * (nb - max_exact)).astype(jnp.int32)
    large = jnp.minimum(large, nb - 1)
    return side + jnp.where(n < max_exact, n, large)

def dilated_window_attention(xn, w_qkv, w_o, rel_bias):
    B, S, _ = xn.shape
    nblk = S // BLOCK
    starts = jnp.arange(nblk, dtype=jnp.int32) * BLOCK
    qkv = xn @ w_qkv
    q, k, v = jnp.split(qkv, 3, axis=-1)
    q = q.reshape(B, S, A_HEADS, HEAD_DIM) * (HEAD_DIM ** -0.5)
    k = k.reshape(B, S, A_HEADS, HEAD_DIM)
    v = v.reshape(B, S, A_HEADS, HEAD_DIM)
    outs, glses = [], []
    h0 = 0
    for (win, dil, nh) in A_GROUPS:
        qg, kg, vg = q[:, :, h0:h0 + nh], k[:, :, h0:h0 + nh], v[:, :, h0:h0 + nh]
        n_side = win // (2 * dil)
        offs = jnp.arange(-n_side, n_side + 1, dtype=jnp.int32) * dil
        bias = rel_bias[t5_bucket(offs), h0:h0 + nh].astype(jnp.float32).T
        qb = qg.reshape(B, nblk, BLOCK, nh, HEAD_DIM).transpose(1, 0, 2, 3, 4)

        def block_fn(args, kg=kg, vg=vg, offs=offs, bias=bias):
            q_blk, start = args
            pos = start + jnp.arange(BLOCK, dtype=jnp.int32)[:, None] + offs[None, :]
            valid = (pos >= 0) & (pos < S)
            idx = jnp.clip(pos, 0, S - 1)
            k_sel = kg[:, idx]
            v_sel = vg[:, idx]
            logits = jnp.einsum('bqhd,bqkhd->bhqk', q_blk, k_sel).astype(jnp.float32)
            logits = logits + bias[None, :, None, :]
            logits = jnp.where(valid[None, None], logits, -jnp.inf)
            lse = jax.nn.logsumexp(logits, axis=-1)
            p = jnp.exp(logits - lse[..., None])
            o = jnp.einsum('bhqk,bqkhd->bqhd', p.astype(vg.dtype), v_sel)
            return o, lse

        o, lse = lax.map(block_fn, (qb, starts))
        o = o.transpose(1, 0, 2, 3, 4).reshape(B, S, nh, HEAD_DIM)
        lse = lse.transpose(1, 0, 3, 2).reshape(B, S, nh)
        outs.append(o)
        glses.append(jax.nn.logsumexp(lse, axis=-1) - math.log(nh))
        h0 += nh
    alpha = jax.nn.softmax(jnp.stack(glses, axis=-1), axis=-1)
    n_groups = len(A_GROUPS)
    o = jnp.concatenate(
        [outs[g] * (n_groups * alpha[..., g])[..., None, None].astype(outs[g].dtype)
         for g in range(n_groups)], axis=2)
    return o.reshape(B, S, A_HEADS * HEAD_DIM) @ w_o

def differential_attention(xn, w_qkv, lam, subln_g, w_o, rel_bias, lambda_init):
    B, S, _ = xn.shape
    nblk = S // BLOCK
    starts = jnp.arange(nblk, dtype=jnp.int32) * BLOCK
    qkv = xn @ w_qkv
    q, k, v = jnp.split(qkv, 3, axis=-1)
    q = q.reshape(B, S, B_HEADS, 2, HEAD_DIM) * (HEAD_DIM ** -0.5)
    k = k.reshape(B, S, B_HEADS, 2, HEAD_DIM)
    v = v.reshape(B, S, B_HEADS, 2 * HEAD_DIM)
    lamf = lam.astype(jnp.float32)
    lam_full = (jnp.exp(jnp.sum(lamf[0] * lamf[1])) - jnp.exp(jnp.sum(lamf[2] * lamf[3]))
                + lambda_init)
    keys = jnp.arange(S, dtype=jnp.int32)
    qb = q.reshape(B, nblk, BLOCK, B_HEADS, 2, HEAD_DIM).transpose(1, 0, 2, 3, 4, 5)

    def block_fn(args):
        q_blk, start = args
        rel = keys[None, :] - (start + jnp.arange(BLOCK, dtype=jnp.int32))[:, None]
        bias = rel_bias[t5_bucket(rel)].astype(jnp.float32)
        bias = bias.reshape(BLOCK, S, B_HEADS, 2).transpose(2, 3, 0, 1)
        logits = jnp.einsum('bqhjd,bkhjd->bhjqk', q_blk, k).astype(jnp.float32) + bias[None]
        p = jax.nn.softmax(logits, axis=-1)
        a = p[:, :, 0] - lam_full * p[:, :, 1]
        return jnp.einsum('bhqk,bkhe->bqhe', a.astype(v.dtype), v)

    o = lax.map(block_fn, (qb, starts))
    o = o.transpose(1, 0, 2, 3, 4).reshape(B, S, B_HEADS, 2 * HEAD_DIM)
    o = rms_norm_2(o, subln_g) * (1.0 - lambda_init)
    return o.reshape(B, S, B_HEADS * 2 * HEAD_DIM) @ w_o

def axial_rope_tables(S):
    n_rows = S // GRID_W
    row = jnp.repeat(jnp.arange(n_rows, dtype=jnp.int32), GRID_W).astype(jnp.float32)
    col = jnp.tile(jnp.arange(GRID_W, dtype=jnp.int32), n_rows).astype(jnp.float32)
    half = AXIS_ROPE_DIM // 2
    inv = ROPE_THETA ** (-jnp.arange(half, dtype=jnp.float32) / half)
    ang = jnp.concatenate([row[:, None] * inv, col[:, None] * inv], axis=-1)
    return jnp.cos(ang), jnp.sin(ang)

def apply_axial_rope(x, cos, sin):
    B, S, H, _ = x.shape
    half = AXIS_ROPE_DIM // 2
    xs = x.astype(jnp.float32).reshape(B, S, H, 2, 2, half)
    x1, x2 = xs[..., 0, :], xs[..., 1, :]
    c = cos.reshape(S, 1, 2, half)
    s = sin.reshape(S, 1, 2, half)
    out = jnp.stack([x1 * c - x2 * s, x2 * c + x1 * s], axis=-2)
    return out.reshape(B, S, H, HEAD_DIM).astype(x.dtype)

def axial_gqa_attention(xn, w_qkv, q_norm_g, k_norm_g, w_o, cos, sin):
    B, S, _ = xn.shape
    nblk = S // BLOCK
    qkv = xn @ w_qkv
    q = qkv[..., :C_HEADS * HEAD_DIM].reshape(B, S, C_HEADS, HEAD_DIM)
    k = qkv[..., C_HEADS * HEAD_DIM:(C_HEADS + C_KV_HEADS) * HEAD_DIM].reshape(B, S, C_KV_HEADS, HEAD_DIM)
    v = qkv[..., (C_HEADS + C_KV_HEADS) * HEAD_DIM:].reshape(B, S, C_KV_HEADS, HEAD_DIM)
    q = apply_axial_rope(rms_norm_2(q, q_norm_g), cos, sin) * (HEAD_DIM ** -0.5)
    k = apply_axial_rope(rms_norm_2(k, k_norm_g), cos, sin)
    qb = q.reshape(B, nblk, BLOCK, C_KV_HEADS, C_GROUP, HEAD_DIM).transpose(1, 0, 2, 3, 4, 5)

    def block_fn(q_blk):
        logits = jnp.einsum('bqkgd,bskd->bkgqs', q_blk, k).astype(jnp.float32)
        p = jax.nn.softmax(logits, axis=-1)
        return jnp.einsum('bkgqs,bskd->bqkgd', p.astype(v.dtype), v)

    o = lax.map(block_fn, qb)
    o = o.transpose(1, 0, 2, 3, 4, 5).reshape(B, S, C_HEADS * HEAD_DIM)
    return o @ w_o

def sq_relu_mlp(xn, w_in, w_out):
    h = jax.nn.relu(xn @ w_in)
    return (h * h) @ w_out

def lambda_init_fn(layer_idx):
    return 0.8 - 0.6 * math.exp(-0.3 * layer_idx)

def second_inputs(seed: int = 0) -> dict:
    key = jax.random.key(seed)
    ks = jax.random.split(key, 24)
    n_a = len(range(0, DEPTH_2, N_MIXERS))
    n_b = len(range(1, DEPTH_2, N_MIXERS))
    n_c = len(range(2, DEPTH_2, N_MIXERS))

    def nrm(k, shape, scale):
        return jax.random.normal(k, shape, jnp.float32) * scale

    d_attn = A_HEADS * HEAD_DIM
    c_qkv = (C_HEADS + 2 * C_KV_HEADS) * HEAD_DIM
    return {
        "x": nrm(ks[0], (BATCH, SEQ, D_MODEL), 1.0),
        "rel_bias": nrm(ks[1], (NUM_BUCKETS, REL_BIAS_HEADS), 0.3),
        "norm_mix_g": 1.0 + nrm(ks[2], (DEPTH_2, D_MODEL), 0.02),
        "norm_mlp_g": 1.0 + nrm(ks[3], (DEPTH_2, D_MODEL), 0.02),
        "norm_final_g": 1.0 + nrm(ks[4], (D_MODEL,), 0.02),
        "a_w_qkv": nrm(ks[5], (n_a, D_MODEL, 3 * d_attn), D_MODEL ** -0.5),
        "a_w_o": nrm(ks[6], (n_a, d_attn, D_MODEL), d_attn ** -0.5),
        "b_w_qkv": nrm(ks[7], (n_b, D_MODEL, 3 * d_attn), D_MODEL ** -0.5),
        "b_lambda": nrm(ks[8], (n_b, 4, HEAD_DIM), 0.1),
        "b_subln_g": 1.0 + nrm(ks[9], (n_b, 2 * HEAD_DIM), 0.02),
        "b_w_o": nrm(ks[10], (n_b, d_attn, D_MODEL), d_attn ** -0.5),
        "c_w_qkv": nrm(ks[11], (n_c, D_MODEL, c_qkv), D_MODEL ** -0.5),
        "c_q_norm_g": 1.0 + nrm(ks[12], (n_c, HEAD_DIM), 0.02),
        "c_k_norm_g": 1.0 + nrm(ks[13], (n_c, HEAD_DIM), 0.02),
        "c_w_o": nrm(ks[14], (n_c, C_HEADS * HEAD_DIM, D_MODEL), (C_HEADS * HEAD_DIM) ** -0.5),
        "mlp_w_in": nrm(ks[15], (DEPTH_2, D_MODEL, D_FF), D_MODEL ** -0.5),
        "mlp_w_out": nrm(ks[16], (DEPTH_2, D_FF, D_MODEL), D_FF ** -0.5),
    }

def second_block(x, rel_bias, norm_mix_g, norm_mlp_g, norm_final_g, a_w_qkv, a_w_o,
              b_w_qkv, b_lambda, b_subln_g, b_w_o, c_w_qkv, c_q_norm_g, c_k_norm_g,
              c_w_o, mlp_w_in, mlp_w_out):
    S = x.shape[1]
    cos, sin = axial_rope_tables(S)
    h = x
    for i in range(DEPTH_2):
        kind, j = i % N_MIXERS, i // N_MIXERS
        hn = rms_norm_2(h, norm_mix_g[i])
        if kind == 0:
            mix = dilated_window_attention(hn, a_w_qkv[j], a_w_o[j], rel_bias)
        elif kind == 1:
            mix = differential_attention(hn, b_w_qkv[j], b_lambda[j], b_subln_g[j], b_w_o[j],
                                         rel_bias, lambda_init_fn(i))
        else:
            mix = axial_gqa_attention(hn, c_w_qkv[j], c_q_norm_g[j], c_k_norm_g[j], c_w_o[j],
                                      cos, sin)
        h = h + mix
        h = h + sq_relu_mlp(rms_norm_2(h, norm_mlp_g[i]), mlp_w_in[i], mlp_w_out[i])
    return rms_norm_2(h, norm_final_g)


def setup_inputs(seed=0):
    out = dict(first_inputs(seed))
    for name, value in second_inputs(seed + 1).items():
        if name != "x":
            out[name + "_2"] = value
    return out


def reference(
    x, c, ada_w, ada_b, norm1_g, w_in, lb_logits, hg_norm_g, w_a, conv_w, conv_b, conv_ln_g,
    conv_ln_b, w_b, w_out, norm2_g, peer_wq, peer_keys, peer_u, peer_v, final_g, rel_bias_2,
    norm_mix_g_2, norm_mlp_g_2, norm_final_g_2, a_w_qkv_2, a_w_o_2, b_w_qkv_2, b_lambda_2,
    b_subln_g_2, b_w_o_2, c_w_qkv_2, c_q_norm_g_2, c_k_norm_g_2, c_w_o_2, mlp_w_in_2,
    mlp_w_out_2,
):
    x = first_block(
        x, c, ada_w, ada_b, norm1_g, w_in, lb_logits, hg_norm_g, w_a, conv_w, conv_b, conv_ln_g,
        conv_ln_b, w_b, w_out, norm2_g, peer_wq, peer_keys, peer_u, peer_v, final_g,
    )
    return second_block(
        x, rel_bias_2, norm_mix_g_2, norm_mlp_g_2, norm_final_g_2, a_w_qkv_2, a_w_o_2,
        b_w_qkv_2, b_lambda_2, b_subln_g_2, b_w_o_2, c_w_qkv_2, c_q_norm_g_2, c_k_norm_g_2,
        c_w_o_2, mlp_w_in_2, mlp_w_out_2,
    )


_drawn_inputs = setup_inputs


def setup_inputs(seed=0):
    import zlib

    import numpy as np

    out = dict(_drawn_inputs(seed))
    spreads = {}
    factors = {'ada_b': 2.876,
     'norm1_g': 6.731,
     'hg_norm_g': 8.0,
     'conv_b': 7.927,
     'conv_ln_g': 8.0,
     'conv_ln_b': 8.0,
     'norm2_g': 6.133,
     'norm_mix_g_2': 4.848,
     'norm_final_g_2': 8.237,
     'b_lambda_2': 4.903,
     'b_subln_g_2': 46.441,
     'norm_mlp_g_2': 3.424}
    for name, (base, spread) in spreads.items():
        noise = np.random.default_rng([zlib.crc32(name.encode()), seed]).standard_normal(out[name].shape)
        drawn = base * np.exp(spread * noise) if base else spread * noise
        out[name] = jnp.asarray(drawn.astype(out[name].dtype))
    for name, factor in factors.items():
        out[name] = (out[name] * factor).astype(out[name].dtype)
    return out
```

```python
from contextlib import ExitStack, contextmanager

import numpy as np

import concourse.bass as bass
from concourse import mybir
from concourse.alu_op_type import AluOpType as ALU

P = 128
T = 512
D = 1024
KT = D // P
TT = T // P
EPS = 1e-6
HEADS = 8
CONV_K = 31
LEVELS = (64, 32, 16, 8, 4, 2, 1)
PEER_HEADS, NKEYS, TOPK = 8, 128, 16
SLOTS = PEER_HEADS * TOPK
A_HEADS = 16
A_GROUPS = ((128, 1, 6), (512, 4, 5), (2048, 16, 5))
B_HEADS = 8
LAMBDA_INIT = 0.8 - 0.6 * float(np.exp(-0.3))
NEG = -1.0e30
LOWEST = -3.0e38
STRIP = T + (TT - 1) * P
RING = 8
BANKS = 4

Q_ADA1, Q_HEADS, Q_GATES, Q_WA, Q_WB, Q_WOUT, Q_WQ, Q_PEER = 0, 2, 6, 14, 15, 16, 17, 19
Q_QKV_A, Q_WO_A, Q_MLP_A = 51, 54, 55
Q_QKV_B, Q_WO_B, Q_MLP_B, Q_END = 63, 66, 67, 75

COLS = {}
_n = 0
for _name, _w in (("c", 8), ("ada_b", 48), ("norm1", 8), ("lb0", 8), ("lb1", 8), ("hgn", 8), ("conv_w", 8 * CONV_K),
                  ("conv_b", 8), ("ln_g", 8), ("ln_b", 8), ("norm2", 8), ("final", 8), ("mix0", 8), ("mix1", 8),
                  ("mlp0", 8), ("mlp1", 8), ("final2", 8), ("subln", 1)):
    COLS[_name] = _n
    _n += _w
NCOLS = _n
RS_NORM = (0, 10, 11, 12, 13, 14, 23, 24)
RS_HEAD, RS_LN, RS_B = 1, 9, 15


class Steps:

    def __init__(self, eng, sem):
        self.eng, self.sem, self.count, self.regs = eng, sem, 0, []

    def value(self):
        v = self.count
        for reg, per in self.regs:
            v = reg * per + v
        return v

    def mark(self, ins):
        ins.then_inc(self.sem, 1)
        self.count += 1

    def wait(self):
        self.eng.wait_ge(self.sem, self.value())

    def done(self, ins):
        self.mark(ins)
        self.wait()

    @contextmanager
    def loop(self, n, per):
        at = self.count
        with self.eng.Fori(0, n) as i:
            self.regs.append((i, per))
            yield i
            self.regs.pop()
        assert self.count - at == per, (self.count - at, per)
        self.count = at + n * per


def build(nc, panels, xT, cols, consts, lmask, keysT, oh, rel, blam, outT, gdram, btab, strips_dram):
    F32 = mybir.dt.float32
    U32 = mybir.dt.uint32
    ACT = mybir.ActivationFunctionType
    AX = mybir.AxisListType
    v_, s_, g_, t_ = nc.vector, nc.scalar, nc.gpsimd, nc.tensor
    ctx = ExitStack()
    with ctx:
        def sb(name, shape, dt=F32):
            return ctx.enter_context(nc.sbuf_tensor(name, shape, dt))

        def sem(name):
            return ctx.enter_context(nc.semaphore(name))

        ps = ctx.enter_context(nc.psum_tensor("ps", [P, 8, 512], F32))
        hT = sb("hT", [P, KT, T])
        uT = sb("uT", [P, KT, T])
        ring = sb("ring", [P, RING, KT, P])
        sq = sb("sq", [P, KT, T])
        st = sb("st", [P, 4, T])
        ms, sr, rt, rstd = (st[:, n, :] for n in range(4))
        cc = sb("cc", [P, NCOLS])
        cst = sb("cst", [P, 2 * P])
        ones = sb("ones", [P, P])
        rbs = sb("rbs", [35, 16])
        ada = sb("ada", [P, 48])
        small = sb("small", [P, 96])
        arena = sb("arena", [P, 27520])
        ident, iota = cst[:, 0:P], cst[:, P:2 * P]

        def view(at, *shape):
            n = int(np.prod(shape))
            a = arena[:, at:at + n]
            if len(shape) == 1:
                return a
            names = "abcd"[:len(shape)]
            return a.rearrange("p (" + " ".join(names) + ") -> p " + " ".join(names),
                               **{names[k]: shape[k] for k in range(1, len(shape))})

        og, cv, sga, sgb = (view(4096 * n, KT, T) for n in range(4))
        at = 4096
        ohs = arena[0:35, 20000:22048].rearrange("p (a b) -> p a b", a=2)
        gtab = arena[0:16, 23000:25048].rearrange("p (a b) -> p a b", a=2)
        lm = arena[:, 18944:19968].bitcast(U32).rearrange("p (a b) -> p a b", a=8)
        osc = view(25100, T)
        lam = view(25700, 4, 64)
        lamt = view(25956, 64)
        qb = view(at, 2, T)
        kb = view(at + 1024, 2, T)
        vb = view(at + 2048, 2, TT, P)
        gb = view(at + 3072, 2, T)
        eb = view(at + 4096, T)
        fb = view(at + 4608, T)
        lf = view(at + 5120, T)
        bb = view(at + 5632, T)
        eq = view(at + 6144, T)
        ek = view(at + 6656, T)
        qoff = view(at + 7168, 4, P)
        koff = view(at + 7680, 4, P)
        db = view(at + 8192, 2, T)
        sd = view(at + 9216, 2, TT, P)
        soff = view(at + 10240, 2, 6, P)
        ob = view(at + 11776, T)
        osq = view(at + 12288, T)
        sg = view(16384, 2, T)
        glu = view(16384 + 1024, T + 32)
        mu = view(16384 + 2048, T)
        qpeer = view(0, 16, T)
        gbuf = view(8192, NKEYS, P)
        ky = view(8192, 16, P)
        srep = view(26624, P)
        arng = st[:, 0:2, :].rearrange("p a (b c) -> p (a b) c", c=P)
        brng = st[:, 2:4, :].rearrange("p a (b c) -> p (a b) c", c=P)
        tk = 26752
        sc16, ix16 = view(tk, 16, TOPK), view(tk + 512, 16, TOPK)
        ix16u = arena[:, tk + 256:tk + 512].bitcast(U32).rearrange("p (a b) -> p a b", b=TOPK)
        cand = sq[:, 0:4, :].rearrange("p k t -> p (k t)")
        oneh = sq[:, 4:8, :].rearrange("p k t -> p (k t)")
        tops = sb("tops", [P, PEER_HEADS, TOPK])
        posu = sb("posu", [P, SLOTS], U32)
        piu = sb("piu", [P, 2, SLOTS], U32)
        pif = sb("pif", [P, 2, SLOTS])
        slot = sb("slot", [P, 3, SLOTS])
        slotT = sb("slotT", [P, 3, P])
        srt = sb("srt", [P, 256])
        gsum = sb("gsum", [P, PEER_HEADS, 2])
        crep = srt[:, 0:256]
        hid = view(0, 2, KT, T)
        gel = view(8192, 4, T)
        gi = view(10240, 2, KT, T)
        qT, kT, vT = (view(4096 * n, KT, T) for n in range(3))
        vtok = view(8192, TT, D)
        pb = view(12288, 2, 2, TT, T)
        strip = view(20480, 2, STRIP)
        pt = view(22272, 2, TT, T)
        qs = sq[:, 3:5, :]
        ks = sq[:, 5:7, :]
        vs = view(26368, 2, TT, P)
        zs = slot[:, :, 0:A_HEADS * TT].rearrange("p a (b c) -> p a b c", c=TT)
        wg = sb("wg", [P, 3, TT])
        gm = sb("gm", [P, 4, TT])
        nm = sb("nm", [P, 2, TT])
        rz = sb("rz", [P, 2, TT])
        mx = sb("mx", [P, 2, TT])
        zt = sb("zt", [P, 2, TT])
        gm0 = sb("gm0", [P, TT])
        lbt = sb("lbt", [P, 24])
        lamc = sb("lamc", [P, 4])
        subc = sb("subc", [P, 1])
        alb = view(12288, 3, T)

        w_slot = [sem(f"w_slot{i}") for i in range(RING)]
        gemm_done = sem("gemm_done")
        bank_free = [sem(f"bank_free{i}") for i in range(BANKS)]
        x_in, c_in = sem("x_in"), sem("c_in")
        act_step, dve_step, pool_step = sem("act_step"), sem("dve_step"), sem("pool_step")
        setup = sem("setup")
        sq_ready, u_ready = sem("sq_ready"), sem("u_ready")
        stat_done, rs_ms, rs_sqrt = sem("stat_done"), sem("rs_ms"), sem("rs_sqrt")
        silu_c, ada_done = sem("silu_c"), sem("ada_done")
        strips_out = sem("strips_out")
        tab_done, tab_sb, tab_dram = sem("tab_done"), sem("tab_sb"), sem("tab_dram")
        lb_sem = sem("lb_sem")
        f_ready, lf_ready, b_ready, ek_ready = sem("f_ready"), sem("lf_ready"), sem("b_ready"), sem("ek_ready")
        off_ready, off_done, soff_ready = sem("off_ready"), sem("off_done"), sem("soff_ready")
        d_ready, e_ready, x_ready = sem("d_ready"), sem("e_ready"), sem("x_ready")
        lvl_done, lvl_evac, v_free = sem("lvl_done"), sem("lvl_evac"), sem("v_free")
        o_copied, osq_ready, og_ready = sem("o_copied"), sem("osq_ready"), sem("og_ready")
        cv_ready, mean_done, xc_ready, cvn_ready, cvs_ready = (sem(n) for n in (
            "cv_ready", "mean_done", "xc_ready", "cvn_ready", "cvs_ready"))
        m_ready, lnsq_ready, upre = sem("m_ready"), sem("lnsq_ready"), sem("upre")
        sc_done, sc_sb, ky_in = sem("sc_done"), sem("sc_sb"), sem("ky_in")
        gate_in, gate_exp, slot_ready, slot_tr, slot_sb = (sem(n) for n in (
            "gate_in", "gate_exp", "slot_ready", "slot_tr", "slot_sb"))
        hot_ready, gmm_done, g_evac, g_out = (sem(n) for n in (
            "hot_ready", "gmm_done", "g_evac", "g_out"))
        g_in = [sem(f"g_in{i}") for i in range(2)]
        hid_ready = [sem(f"hid_ready{i}") for i in range(3)]
        strip_in = [[sem(f"strip_in{s}{i}") for i in range(2)] for s in range(2)]
        att = []
        for s in range(2):
            att.append({n: sem(f"{n}_{s}") for n in (
                "staged", "lg_done", "nm_ready", "p_ready", "pn_ready", "tr_done", "pt_ready", "av_done",
                "o_ready", "oT_ready", "lse")})
        al_ready, alb_done, alb_sb = sem("al_ready"), sem("alb_done"), sem("alb_sb")
        bsq_ready = sem("bsq_ready")
        out_done, carried = sem("out_done"), sem("carried")

        block = ctx.enter_context(nc.Block())

        def col(name, k=0):
            return cc[:, COLS[name] + k:COLS[name] + k + 1]

        def colr(name, k, stride=1, n=1):
            return cc[:, bass.ds(k * stride + COLS[name] + n - 1, 1)]

        @block.sync
        def _(sp):
            for j in range(RING):
                sp.dma_start(ring[:, j], panels[j]).then_inc(w_slot[j], 16)
            with sp.Fori(0, Q_END - 1) as i:
                for j in range(RING):
                    sp.wait_ge(gemm_done, i * RING + (j + 1))
                    sp.dma_start(ring[:, j], panels[i * RING + (RING + j)]).then_inc(w_slot[j], 16)
            sp.wait_ge(u_ready, 64)
            sp.dma_start(outT, uT[:]).then_inc(out_done, 16)
            sp.wait_ge(out_done, 16)

        @block.tensor
        def _(pe):
            def start_panel(q8, j):
                pe.wait_ge(w_slot[j % RING], q8 * 16 + 16 * (j // RING + 1))
                if not (isinstance(q8, int) and q8 * 2 + j // BANKS == 0):
                    pe.wait_ge(bank_free[j % BANKS], q8 * 2 + j // BANKS)

            def panel(q8, j, X, n=T):
                start_panel(q8, j)
                for k in range(KT):
                    last = t_.matmul(ps[:, j % BANKS, 0:n], ring[:, j % RING, k, :], X[:, k, 0:n],
                                     start=(k == 0), stop=(k == KT - 1))
                last.then_inc(gemm_done, 1)

            def panel_tok(q8, j, X):
                start_panel(q8, j)
                for tt in range(TT):
                    for k in range(KT):
                        last = t_.matmul(ps[:, j % BANKS, tt * P:(tt + 1) * P], X[:, k, tt * P:(tt + 1) * P],
                                         ring[:, j % RING, k, :], start=(k == 0), stop=(k == KT - 1))
                last.then_inc(gemm_done, 1)

            def stat(idx, tiles, ready, at):
                if idx:
                    pe.wait_ge(rs_ms, idx)
                for k, tile in enumerate(tiles):
                    pe.wait_ge(ready, at + k + 1)
                    last = t_.matmul(ps[:, 4, :], ones[:], tile, start=(k == 0), stop=(k == len(tiles) - 1))
                last.then_inc(stat_done, 1)

            def norm(r):
                stat(RS_NORM[r], [sq[:, k, :] for k in range(KT)], sq_ready, KT * r)
                pe.wait_ge(u_ready, KT * (r + 1))

            pe.wait_ge(c_in, 16 * 6)
            for tab in range(2):
                for half in range(2):
                    last = t_.matmul(ps[0:16, 4 + 2 * tab + half, :], rbs[:], ohs[:, tab, half * 512:half * 512 + 512],
                                     start=True, stop=True)
            last.then_inc(tab_done, 1)
            pe.wait_ge(silu_c, 1)
            for j in range(16):
                panel(j // 8, j % 8, small[:, 0:8].rearrange("p (k a) -> p k a", a=1), 1)
            pe.wait_ge(tab_sb, 4)
            norm(0)

            def head_off(h):
                pe.wait_ge(lvl_evac, h * 8 + 1)
                pe.wait_ge(o_copied, h * 1 + 1)
                pe.wait_ge(off_ready, h * 1 + 1)
                t_.matmul(ps[:, 5, 0:P], koff[:, 0, :], qoff[:, 0, :], start=True, stop=True)
                t_.matmul(ps[:, 5, P:2 * P], koff[:, 2, :], qoff[:, 3, :], start=True, stop=True).then_inc(off_done, 1)
                t_.matmul(ps[:, 6, 0:2 * P], koff[:, 3, :], qoff[:, 1:3, :], start=True, stop=True)
                t_.matmul(ps[:, 6, 2 * P:4 * P], koff[:, 1, :], qoff[:, 1:3, :], start=True, stop=True).then_inc(off_done, 1)

            def head_level(h, hh, n):
                bank = 7 if n % 2 == 0 else 5
                if n == 1:
                    pe.wait_ge(soff_ready, h * 2 + 1)
                elif n >= 2:
                    pe.wait_ge(lvl_evac, h * 8 + n)
                if n < 7:
                    pe.wait_ge(x_ready, h * 7 + (n + 1))
                for tt in range(TT):
                    if n < 7:
                        a = b = sq[:, n, tt * P:(tt + 1) * P]
                    else:
                        a, b = kb[:, hh, tt * P:(tt + 1) * P], qb[:, hh, tt * P:(tt + 1) * P]
                    last = t_.matmul(ps[:, bank, tt * P:(tt + 1) * P], a, b, start=True, stop=True)
                last.then_inc(lvl_done, 1)

            PAIRS = {(0, 1): 0, (2, 3): 1, (0, 2): 2, (0, 3): 3, (1, 2): 4, (1, 3): 5}

            def head_pv(h, hh):
                pe.wait_ge(soff_ready, h * 2 + 2)
                pe.wait_ge(lvl_evac, h * 8 + 9)
                for j in range(TT):
                    for i in range(j + 1):
                        S = sd[:, hh, j, :] if i == j else soff[:, hh, PAIRS[i, j], :]
                        last = t_.matmul(ps[:, 6, j * P:(j + 1) * P], vb[:, hh, i, :], S, start=(i == 0), stop=(i == j))
                last.then_inc(v_free, 1)

            def head_stat(h):
                pe.wait_ge(rs_ms, h * 1 + RS_HEAD)
                pe.wait_ge(osq_ready, h * 1 + 1)
                t_.matmul(ps[:, 4, :], ones[:], osq[:], start=True, stop=True).then_inc(stat_done, 1)

            def head_gemm(q8, j0, n):
                if n == 2:
                    panel_tok(q8, j0 + 2, uT)
                else:
                    panel(q8, j0 + n, uT)

            def head_step(h, hh, q8n, jn):
                nxt = q8n is not None
                if nxt:
                    head_gemm(q8n, jn, 0)
                    head_gemm(q8n, jn, 1)
                head_off(h)
                head_level(h, hh, 0)
                head_level(h, hh, 1)
                if nxt:
                    head_gemm(q8n, jn, 2)
                for n in (2, 3, 4):
                    head_level(h, hh, n)
                if nxt:
                    head_gemm(q8n, jn, 3)
                for n in (5, 6, 7):
                    head_level(h, hh, n)
                head_pv(h, hh)
                head_stat(h)

            for n in range(4):
                head_gemm(Q_HEADS, 0, n)
            with pe.Fori(0, HEADS // 2 - 1) as i:
                head_step(i * 2, 0, i + Q_HEADS, 4)
                head_step(i * 2 + 1, 1, i + (Q_HEADS + 1), 0)
            head_step(6, 0, Q_HEADS + 3, 4)
            head_step(7, 1, None, None)

            cvec = small[:, 0:8].rearrange("p (k a) -> p k a", a=1)
            with pe.Fori(0, KT) as i:
                for j in range(8):
                    if j in (0, 1, 3, 5):
                        panel(i + Q_GATES, j, uT)
                    else:
                        panel(i + Q_GATES, j, cvec, 1)
            for k in range(KT):
                pe.wait_ge(cv_ready, k + 1)
                last = t_.matmul(ps[:, 5, :], ones[:], cv[:, k, :], start=(k == 0), stop=(k == KT - 1))
            last.then_inc(mean_done, 1)
            pe.wait_ge(og_ready, HEADS + 1)
            for j in range(KT):
                panel(Q_WA, j, og)
            stat(RS_LN, [sq[:, k, :] for k in range(KT)], lnsq_ready, 0)
            pe.wait_ge(cvs_ready, KT)
            for j in range(KT):
                panel(Q_WB, j, cv)
            pe.wait_ge(m_ready, KT)
            for j in range(KT):
                panel(Q_WOUT, j, sga)
            norm(1)

            for j in range(16):
                panel(Q_WQ + j // 8, j % 8, uT)
            for b in range(BANKS):
                pe.wait_ge(bank_free[b], 2 * (Q_WQ + 2))
            pe.wait_ge(ky_in, 16)
            for hp in range(16):
                if hp >= 4:
                    pe.wait_ge(sc_sb, hp - 3)
                for tt in range(TT):
                    last = t_.matmul(ps[:, hp % 4, tt * P:(tt + 1) * P], qpeer[:, hp, tt * P:(tt + 1) * P], ky[:, hp, :],
                                     start=True, stop=True)
                last.then_inc(sc_done, 1)
            for tt in range(TT):
                pe.wait_ge(slot_ready, 3 * (tt + 1))
                for n in range(3):
                    last = t_.transpose(ps[:, 4, n * P:(n + 1) * P], slot[:, n, :], ident)
                last.then_inc(slot_tr, 1)
                with pe.Fori(0, 16) as i:
                    for par in range(2):
                        n = i * 2 + (tt * 32 + par)
                        pe.wait_ge(hot_ready, n * 1 + 1)
                        pe.wait_ge(g_evac, n * 1 + 1)
                        for k in range(4):
                            last = t_.matmul(ps[:, 6 + par, k * P:(k + 1) * P], brng[:, 4 * par + k, :],
                                             arng[:, 4 * par + k, :], start=True, stop=True)
                        last.then_inc(gmm_done, 1)
            pe.wait_ge(sc_sb, 16)
            pe.wait_ge(g_evac, 130)

            def hidden(s, q8, groups):
                def up(q, g):
                    for j in range(8):
                        panel(q, j, uT)

                def down(q, par, g):
                    pe.wait_ge(hid_ready[s], g * 8 + 8)
                    for j in range(8):
                        panel(q, j, hid[:, par])

                up(q8, 0)
                with pe.Fori(0, groups // 2 - 1) as i:
                    up(i * 4 + (q8 + 1), None)
                    down(i * 4 + (q8 + 2), 0, i * 2)
                    up(i * 4 + (q8 + 3), None)
                    down(i * 4 + (q8 + 4), 1, i * 2 + 1)
                e = q8 + 2 * groups - 3
                up(e, None)
                down(e + 1, 0, groups - 2)
                down(e + 2, 1, groups - 1)

            hidden(0, Q_PEER, 16)
            norm(2)

            def attention(s, r, q_qkv, q_wo):
                a = att[s]
                norm(r)
                for j in range(16):
                    panel(q_qkv + j // 8, j % 8, uT)
                for j in range(8):
                    panel_tok(q_qkv + 2, j, uT)
                for b in range(BANKS):
                    pe.wait_ge(bank_free[b], 2 * (q_qkv + 3))

                def logits(n, par, hh):
                    pe.wait_ge(a["staged"], n * 3 + 3)
                    for qt in range(TT):
                        if not (isinstance(n, int) and n * 8 + 4 * hh + qt < 4):
                            pe.wait_ge(a["nm_ready"], n * 8 + (4 * hh + qt - 3))
                        t_.matmul(ps[:, qt, :], qs[64 * hh:64 * hh + 64, par, qt * P:(qt + 1) * P],
                                  ks[64 * hh:64 * hh + 64, par, :], start=True, stop=True).then_inc(a["lg_done"], 1)

                def values(n, par, hh, u, src):
                    for qt in range(TT):
                        pe.wait_ge(a["pn_ready"], u * 4 + (qt + 1))
                        pe.wait_ge(a["pt_ready"], u * 4 + (qt + 1))
                        for kt in range(TT):
                            last = t_.transpose(ps[:, 4 + qt % 2, kt * P:(kt + 1) * P],
                                                pb[:, par, src, qt, kt * P:(kt + 1) * P], ident)
                        last.then_inc(a["tr_done"], 1)
                    pe.wait_ge(a["pt_ready"], u * 4 + 6)
                    pe.wait_ge(a["o_ready"], u * 1 + 1)
                    bank = 6 + (hh if s == 0 else 0)
                    for kt in range(TT):
                        last = t_.matmul(ps[:, bank, :], vs[:, par, kt, :], pt[:, hh if s == 0 else par, kt, :],
                                         start=(kt == 0), stop=(kt == TT - 1))
                    last.then_inc(a["av_done"], 1)

                def bstat(u):
                    pe.wait_ge(rs_ms, u * 1 + RS_B)
                    pe.wait_ge(bsq_ready, u * 1 + 1)
                    t_.matmul(ps[:, 7, :], ones[:], sq[:, 0, :], start=True, stop=True).then_inc(stat_done, 1)

                if s == 0:
                    logits(0, 0, 0)
                    with pe.Fori(0, 3) as i:
                        logits(i * 2, 0, 1)
                        values(i * 2, 0, 0, i * 4, 0)
                        logits(i * 2 + 1, 1, 0)
                        values(i * 2, 0, 1, i * 4 + 1, 1)
                        logits(i * 2 + 1, 1, 1)
                        values(i * 2 + 1, 1, 0, i * 4 + 2, 0)
                        logits(i * 2 + 2, 0, 0)
                        values(i * 2 + 1, 1, 1, i * 4 + 3, 1)
                    logits(6, 0, 1)
                    values(6, 0, 0, 12, 0)
                    logits(7, 1, 0)
                    values(6, 0, 1, 13, 1)
                    logits(7, 1, 1)
                    values(7, 1, 0, 14, 0)
                    values(7, 1, 1, 15, 1)
                    pe.wait_ge(al_ready, 1)
                    for g in range(3):
                        for qt in range(TT):
                            last = t_.matmul(ps[:, g, qt * P:(qt + 1) * P], wg[:, g, qt:qt + 1].to_broadcast([P, P]), ident,
                                             start=True, stop=True)
                    last.then_inc(alb_done, 1)
                else:
                    logits(0, 0, 0)
                    logits(0, 0, 1)
                    with pe.Fori(0, 3) as i:
                        logits(i * 2 + 1, 1, 0)
                        logits(i * 2 + 1, 1, 1)
                        values(None, 0, 0, i * 2, 0)
                        bstat(i * 2)
                        logits(i * 2 + 2, 0, 0)
                        logits(i * 2 + 2, 0, 1)
                        values(None, 1, 0, i * 2 + 1, 0)
                        bstat(i * 2 + 1)
                    logits(7, 1, 0)
                    logits(7, 1, 1)
                    values(None, 0, 0, 6, 0)
                    bstat(6)
                    values(None, 1, 0, 7, 0)
                    bstat(7)
                pe.wait_ge(a["oT_ready"], 16 if s == 0 else 8)
                for j in range(8):
                    panel(q_wo, j, uT)

            attention(0, 3, Q_QKV_A, Q_WO_A)
            norm(4)
            hidden(1, Q_MLP_A, 4)
            attention(1, 5, Q_QKV_B, Q_WO_B)
            norm(6)
            hidden(2, Q_MLP_B, 4)
            norm(7)

        LAST = {1: Q_WOUT, 2: Q_PEER + 31, 4: Q_WO_A, 5: Q_MLP_A + 7, 6: Q_WO_B, 7: Q_MLP_B + 7}

        @block.scalar
        def _(act):
            S = Steps(act, act_step)
            for dst, src in ((cc[:], cols), (cst[:], consts), (ohs, oh), (rbs[:], rel), (lm, lmask),
                             (lam, blam)):
                act.dma_start(dst, src).then_inc(c_in, 16)
            act.dma_start(hT[:], xT).then_inc(x_in, 16)

            def taken(q8, j):
                act.wait_ge(gemm_done, q8 * 8 + (j + 1))

            def root(idx):
                act.wait_ge(rs_ms, idx * 1 + 1 if not isinstance(idx, int) else idx + 1)
                s_.activation(sr[:], ms[:], ACT.Sqrt).then_inc(rs_sqrt, 1)

            def norm(r):
                if r:
                    act.wait_ge(stat_done, RS_NORM[r])
                else:
                    act.wait_ge(x_in, 16)
                for k in range(KT):
                    if r == 3:
                        act.wait_ge(u_ready, KT * 2 + k + 1)
                    elif r:
                        act.wait_ge(bank_free[k % BANKS], 2 * LAST[r] + k // BANKS + 1)
                    s_.activation(sq[:, k, :], hT[:, k, :], ACT.Square).then_inc(sq_ready, 1)
                root(RS_NORM[r])
                if r < 2:
                    for k in range(KT):
                        act.wait_ge(upre, KT * r + k + 1)
                        s_.activation(uT[:, k, :], uT[:, k, :], ACT.Identity,
                                      bias=ada[:, 24 * r + k:24 * r + k + 1]).then_inc(u_ready, 1)

            act.wait_ge(c_in, 16 * 6)
            s_.activation(small[:, 0:8], cc[:, COLS["c"]:COLS["c"] + 8], ACT.Silu).then_inc(silu_c, 1)
            act.wait_ge(tab_done, 1)
            for n in range(4):
                s_.activation(gtab[:, n // 2, (n % 2) * 512:(n % 2) * 512 + 512], ps[0:16, 4 + n, :], ACT.Copy).then_inc(tab_sb, 1)
            act.wait_ge(tab_sb, 4)
            act.dma_start(btab.rearrange("s h x -> h s x"), gtab).then_inc(tab_dram, 16)
            act.wait_ge(lb_sem, 1)
            s_.activation(lbt[:, 0:16], lbt[:, 0:16], ACT.Exp).then_inc(lb_sem, 1)
            for n in range(16):
                taken(n // 8, n % 8)
                s_.activation(ada[:, n:n + 1], ps[:, n % BANKS, 0:1], ACT.Identity, bias=col("ada_b", n)).then_inc(bank_free[n % BANKS], 1)
            norm(0)

            def head(h, hh, q8):
                j0 = 4 * hh
                taken(q8, j0)
                act.wait_ge(f_ready, h * 1 + 1)
                s_.activation(eb[:], ps[:, 0, :], ACT.Exp, scale=-1.0).then_inc(bank_free[0], 1)
                taken(q8, j0 + 1)
                s_.activation(qb[:, hh, :], ps[:, 1, :], ACT.Copy).then_inc(bank_free[1], 1)
                taken(q8, j0 + 2)
                s_.activation(vb[:, hh], ps[:, 2, :].rearrange("p (a b) -> p a b", a=TT), ACT.Copy).then_inc(bank_free[2], 1)
                taken(q8, j0 + 3)
                s_.activation(gb[:, hh, :], ps[:, 3, :], ACT.Silu).then_inc(bank_free[3], 1)
                act.wait_ge(f_ready, h * 1 + 2)
                s_.activation(lf[:], fb[:], ACT.Ln).then_inc(lf_ready, 1)
                act.wait_ge(b_ready, h * 1 + 1)
                s_.activation(eq[:, P:T], bb[:, P:T], ACT.Exp)
                for n in range(3):
                    s_.activation(ek[:, n * P:(n + 1) * P], bb[:, n * P:(n + 1) * P], ACT.Exp, scale=-1.0,
                                  bias=bb[:, n * P + P - 1:n * P + P])
                s_.activation(small[:, 40:42], bb[:, 2 * P - 1:3 * P:P], ACT.Exp).then_inc(ek_ready, 1)
                for n in range(7):
                    act.wait_ge(d_ready, h * 7 + (n + 1))
                    s_.activation(db[:, n % 2, :], db[:, n % 2, :], ACT.Exp).then_inc(e_ready, 1)
                act.wait_ge(off_done, h * 2 + 1)
                s_.activation(soff[:, hh, 0:2, :], ps[:, 5, 0:2 * P].rearrange("p (a b) -> p a b", a=2), ACT.Copy).then_inc(soff_ready, 1)
                act.wait_ge(off_done, h * 2 + 2)
                s_.activation(soff[:, hh, 2:6, :], ps[:, 6, :].rearrange("p (a b) -> p a b", a=4), ACT.Copy).then_inc(soff_ready, 1)
                act.wait_ge(v_free, h * 1 + 3)
                act.wait_ge(og_ready, h * 1 + 1)
                s_.activation(ob[:], ps[:, 6, :], ACT.Copy).then_inc(o_copied, 1)
                act.wait_ge(o_copied, h * 1 + 2)
                s_.activation(osq[:], ob[:], ACT.Square).then_inc(osq_ready, 1)
                act.wait_ge(rs_ms, h * 1 + (RS_HEAD + 1))
                s_.activation(sr[:], ms[:], ACT.Sqrt).then_inc(rs_sqrt, 1)

            with act.Fori(0, HEADS // 2) as i:
                head(i * 2, 0, i + Q_HEADS)
                head(i * 2 + 1, 1, i + Q_HEADS)

            with act.Fori(0, KT) as i:
                q8 = i + Q_GATES
                taken(q8, 0)
                act.wait_ge(bank_free[1], q8 * 2)
                s_.activation(sg[:, 0, :], ps[:, 0, :], ACT.Sigmoid).then_inc(bank_free[0], 1)
                n = 0
                for j in range(2, 8):
                    taken(q8, j)
                    if j in (3, 5):
                        dst = sga if j == 3 else sgb
                        s_.activation(dst[:, bass.ds(i, 1), :], ps[:, j % BANKS, :], ACT.Sigmoid).then_inc(bank_free[j % BANKS], 1)
                    else:
                        s_.activation(ada[:, bass.ds(i * 4 + (16 + n), 1)], ps[:, j % BANKS, 0:1], ACT.Identity,
                                      bias=cc[:, bass.ds(i * 4 + (COLS["ada_b"] + 16 + n), 1)]).then_inc(bank_free[j % BANKS], 1)
                        n += 1
            act.wait_ge(stat_done, RS_LN)
            for k in range(KT):
                act.wait_ge(xc_ready, k + 1)
                s_.activation(sq[:, k, :], cv[:, k, :], ACT.Square).then_inc(lnsq_ready, 1)
            root(RS_LN)
            for k in range(KT):
                act.wait_ge(cvn_ready, k + 1)
                s_.activation(cv[:, k, :], cv[:, k, :], ACT.Silu, bias=col("ln_b", k)).then_inc(cvs_ready, 1)
            norm(1)

            for j in range(16):
                taken(Q_WQ, j)
                s_.activation(qpeer[:, j, :], ps[:, j % BANKS, :], ACT.Copy).then_inc(bank_free[j % BANKS], 1)
            act.dma_start(ky, keysT).then_inc(ky_in, 16)
            act.wait_ge(tab_dram, 16)
            act.dma_start(strips_dram, bass.AP(tensor=btab.tensor, offset=P - 1, ap=[[1024, 2 * A_HEADS], [-1, P], [1, STRIP]]))\
               .then_inc(strips_out, 16)
            for hp in range(16):
                act.wait_ge(sc_done, hp + 1)
                s_.activation(qpeer[:, hp, :], ps[:, hp % 4, :], ACT.Copy).then_inc(sc_sb, 1)
            with act.Fori(0, TT) as tt:
                act.wait_ge(gate_in, tt * 1 + 1)
                s_.activation(slot[:, 2, :], slot[:, 2, :], ACT.Exp).then_inc(gate_exp, 1)
                act.wait_ge(g_out, tt * 64 + 16)
                with act.Fori(0, 16) as i:
                    for par in range(2):
                        act.wait_ge(gmm_done, tt * 32 + i * 2 + (par + 3))
                        s_.activation(gbuf[:, :, bass.ds(i * 8 + 4 * par, 4)].rearrange("p i t -> p t i"),
                                      ps[:, 6 + par, :].rearrange("p (a b) -> p a b", a=4), ACT.Copy).then_inc(g_evac, 1)
                act.wait_ge(g_evac, tt * 32 + 34)
                for c in range(4):
                    act.dma_start(gdram[bass.ds(tt, 1), 32 * c:32 * c + 32].rearrange("s i j t -> j (s i) t"),
                                  gbuf[:, 32 * c:32 * c + 32, :]).then_inc(g_out, 16)
            act.wait_ge(g_out, 272)

            def hidden(s, q8, groups):
                def load(g, par):
                    if s == 0:
                        for k in range(8):
                            act.dma_start(gi[:, par, k, :].rearrange("p (a t) -> p a t", a=TT),
                                          gdram[:, bass.ds(g * 8 + k, 1)].rearrange("a i j t -> j (i a) t")).then_inc(g_in[par], 16)

                def up(q, g, par, first=False, fetch=True):
                    if fetch:
                        if not first and s == 0:
                            act.wait_ge(hid_ready[s], g * 8)
                        load(g + 1, 1 - par)
                    for j in range(8):
                        taken(q, j)
                        if not (first and j < 4):
                            act.wait_ge(hid_ready[s], g * 8 + (j - 3))
                        s_.activation(gel[:, j % 4, :], ps[:, j % BANKS, :], ACT.Gelu if s == 0 else ACT.Relu).then_inc(bank_free[j % BANKS], 1)

                load(0, 0)
                up(q8, 0, 0, first=True)
                with act.Fori(0, groups // 2 - 1) as i:
                    up(i * 4 + (q8 + 1), i * 2 + 1, 1)
                    up(i * 4 + (q8 + 3), i * 2 + 2, 0)
                up(q8 + 2 * groups - 3, groups - 1, 1, fetch=False)

            hidden(0, Q_PEER, 16)
            norm(2)

            def attention(s, r, q_qkv):
                a = att[s]
                norm(r)
                for j in range(24):
                    taken(q_qkv, j)
                    if j < 8:
                        ins = s_.activation(qT[:, j, :], ps[:, j % BANKS, :], ACT.Copy, scale=0.125)
                    elif j < 16:
                        ins = s_.activation(kT[:, j - 8, :], ps[:, j % BANKS, :], ACT.Copy)
                    else:
                        ins = s_.activation(vtok[:, :, (j - 16) * P:(j - 15) * P], ps[:, j % BANKS, :].rearrange("p (a b) -> p a b", a=TT), ACT.Copy)
                    ins.then_inc(bank_free[j % BANKS], 1)
                if s == 0:
                    act.wait_ge(strips_out, 16)

                def strips(u, hh):
                    act.dma_start(strip[:, hh:hh + 1, :], strips_dram[bass.ds(u + s * A_HEADS, 1)].rearrange("u p y -> p u y"))\
                       .then_inc(strip_in[s][hh], 16)

                def exps(n, par, hh, more=True):
                    for qt in range(TT):
                        act.wait_ge(a["nm_ready"], n * 8 + (4 * hh + qt + 1))
                        s_.activation(pb[:, par, hh, qt, :], pb[:, par, hh, qt, :], ACT.Exp, bias=nm[:, hh, qt:qt + 1],
                                      accum_out=zt[:, hh, qt:qt + 1]).then_inc(a["p_ready"], 1)
                    if more:
                        strips(n * 2 + (hh + 2), hh)

                def values(n, par, hh, u):
                    for qt in range(TT):
                        act.wait_ge(a["tr_done"], u * 4 + (qt + 1))
                        s_.activation(pt[:, hh if s == 0 else par, :, qt * P:(qt + 1) * P],
                                      ps[:, 4 + qt % 2, :].rearrange("p (a b) -> p a b", a=TT), ACT.Copy).then_inc(a["pt_ready"], 1)
                    act.wait_ge(a["av_done"], u * 1 + 1)
                    if s == 0:
                        rows = slice(64 * hh, 64 * hh + 64)
                        s_.activation(uT[rows, bass.ds(n, 1), :] if not isinstance(n, int) else uT[rows, n:n + 1, :],
                                      ps[rows, 6 + hh, :], ACT.Copy).then_inc(a["o_ready"], 1)
                    else:
                        s_.activation(sq[:, 1 + par, :], ps[:, 6, :], ACT.Copy).then_inc(a["o_ready"], 1)
                        act.wait_ge(a["o_ready"], u * 1 + 2)
                        act.wait_ge(stat_done, u * 1 + RS_B)
                        s_.activation(sq[:, 0, :], sq[:, 1 + par, :], ACT.Square).then_inc(bsq_ready, 1)
                        act.wait_ge(rs_ms, u * 1 + (RS_B + 1))
                        s_.activation(sr[:], ms[:], ACT.Sqrt).then_inc(rs_sqrt, 1)

                strips(0, 0)
                strips(1, 1)
                if s == 0:
                    exps(0, 0, 0)
                    with act.Fori(0, 3) as i:
                        exps(i * 2, 0, 1)
                        values(i * 2, 0, 0, i * 4)
                        exps(i * 2 + 1, 1, 0)
                        values(i * 2, 0, 1, i * 4 + 1)
                        exps(i * 2 + 1, 1, 1)
                        values(i * 2 + 1, 1, 0, i * 4 + 2)
                        exps(i * 2 + 2, 0, 0)
                        values(i * 2 + 1, 1, 1, i * 4 + 3)
                    exps(6, 0, 1)
                    values(6, 0, 0, 12)
                    exps(7, 1, 0, more=False)
                    values(6, 0, 1, 13)
                    exps(7, 1, 1, more=False)
                    values(7, 1, 0, 14)
                    values(7, 1, 1, 15)
                    act.wait_ge(a["lse"], 1)
                    s_.activation(zs[:, 2], zs[:, 1], ACT.Ln).then_inc(a["lse"], 1)
                    act.wait_ge(a["lse"], 3)
                    s_.activation(zs[:, 1], zs[:, 0], ACT.Exp).then_inc(a["lse"], 1)
                    act.wait_ge(alb_done, 1)
                    for g in range(3):
                        s_.activation(alb[:, g, :], ps[:, g, :], ACT.Copy).then_inc(alb_sb, 1)
                else:
                    exps(0, 0, 0)
                    exps(0, 0, 1)
                    with act.Fori(0, 3) as i:
                        exps(i * 2 + 1, 1, 0)
                        exps(i * 2 + 1, 1, 1)
                        values(None, 0, 0, i * 2)
                        exps(i * 2 + 2, 0, 0)
                        exps(i * 2 + 2, 0, 1)
                        values(None, 1, 0, i * 2 + 1)
                    exps(7, 1, 0, more=False)
                    exps(7, 1, 1, more=False)
                    values(None, 0, 0, 6)
                    values(None, 1, 0, 7)

            attention(0, 3, Q_QKV_A)
            norm(4)
            hidden(1, Q_MLP_A, 4)
            act.wait_ge(lb_sem, 3)
            s_.activation(lamc[:, 0:2], lamc[:, 0:2], ACT.Exp).then_inc(lb_sem, 1)
            attention(1, 5, Q_QKV_B)
            norm(6)
            hidden(2, Q_MLP_B, 4)
            norm(7)

        @block.vector
        def _(ve):
            S = Steps(ve, dve_step)

            def taken(q8, j):
                ve.wait_ge(gemm_done, q8 * 8 + (j + 1))

            def evacuated(q8, j):
                ve.wait_ge(bank_free[j % BANKS], q8 * 2 + (j // BANKS + 1))

            def carry_waits():
                ve.sem_inc(carried, 1)

            def rsqrt(idx, width, bank=4):
                ve.wait_ge(stat_done, idx * 1 + 1 if not isinstance(idx, int) else idx + 1)
                v_.tensor_scalar(ms[:], ps[:, bank, :], 1.0 / width, EPS, ALU.mult, ALU.add).then_inc(rs_ms, 1)
                ve.wait_ge(rs_sqrt, idx * 1 + 1 if not isinstance(idx, int) else idx + 1)
                S.done(v_.reciprocal(rt[:], sr[:]))
                S.done(v_.tensor_tensor(rstd[:], rt[:], rt[:], ALU.mult))
                S.done(v_.tensor_tensor(rstd[:], rstd[:], ms[:], ALU.mult))
                S.done(v_.tensor_scalar(rstd[:], rstd[:], -0.5, 1.5, ALU.mult, ALU.add))
                S.done(v_.tensor_tensor(rstd[:], rstd[:], rt[:], ALU.mult))

            def norm(r, gain):
                rsqrt(RS_NORM[r], D)
                for k in range(KT):
                    out = hT if r == 2 else uT
                    v_.scalar_tensor_tensor(out=out[:, k, :], in0=hT[:, k, :], scalar=gain(k), in1=rstd[:],
                                            op0=ALU.mult, op1=ALU.mult).then_inc(upre if r < 2 else u_ready, 1)

            S.done(v_.memset(ones[:], 1.0))
            S.done(v_.memset(sd[:], 0.0))
            ve.wait_ge(c_in, 16 * 6)
            l0 = cc[:, COLS["lb0"]:COLS["lb0"] + 8]
            l1 = cc[:, COLS["lb1"]:COLS["lb1"] + 8]
            S.done(v_.tensor_tensor(lbt[:, 16:24], l0, l1, ALU.max))
            S.done(v_.tensor_tensor(lbt[:, 0:8], l0, lbt[:, 16:24], ALU.subtract))
            v_.tensor_tensor(lbt[:, 8:16], l1, lbt[:, 16:24], ALU.subtract).then_inc(lb_sem, 1)
            ve.wait_ge(lb_sem, 2)
            S.done(v_.tensor_tensor(lbt[:, 16:24], lbt[:, 0:8], lbt[:, 8:16], ALU.add))
            S.done(v_.reciprocal(lbt[:, 16:24], lbt[:, 16:24]))
            S.done(v_.tensor_tensor(small[:, 8:16], lbt[:, 0:8], lbt[:, 16:24], ALU.mult))
            S.done(v_.tensor_scalar(small[:, 16:24], small[:, 8:16], -1.0, 1.0, ALU.mult, ALU.add))
            for n in range(2):
                S.done(v_.tensor_tensor_reduce(out=lamt[:], in0=lam[:, 2 * n, :], in1=lam[:, 2 * n + 1, :], scale=1.0, scalar=0.0,
                                               op0=ALU.mult, op1=ALU.add, accum_out=lamc[:, n:n + 1]))
            v_.tensor_scalar(subc[:], col("subln"), 1.0 - LAMBDA_INIT, None, ALU.mult).then_inc(lb_sem, 1)

            def gain_of(r):
                name = "norm1" if r == 0 else "norm2"
                S.done(v_.tensor_scalar(small[:, 48:56], ada[:, 24 * r + 8:24 * r + 16], 1.0, None, ALU.add))
                S.done(v_.tensor_tensor(small[:, 24 + 8 * r:32 + 8 * r], small[:, 48:56], cc[:, COLS[name]:COLS[name] + 8], ALU.mult))

            for j in range(4):
                evacuated(1, 4 + j)
            gain_of(0)
            norm(0, lambda k: small[:, 24 + k:25 + k])

            def seg(x, L):
                y = x.rearrange("p (s w) -> p s w", w=2 * L)
                n = T // (2 * L)
                return y[:, :, 0:L], y[:, :, L:2 * L], y[:, :, L - 1:L].broadcast_to([P, n, L])

            def head(h, hh, q8):
                j0 = 4 * hh
                evacuated(q8, j0)
                S.done(v_.tensor_scalar(eb[:], eb[:], 1.0, None, ALU.add))
                S.done(v_.reciprocal(fb[:], eb[:]))
                v_.tensor_scalar(fb[:], fb[:], small[:, bass.ds(h * 1 + 16, 1)], small[:, bass.ds(h * 1 + 8, 1)],
                                 ALU.mult, ALU.add).then_inc(f_ready, 1)
                ve.wait_ge(f_ready, h * 1 + 2)
                S.done(v_.tensor_scalar(kb[:, hh, :], fb[:], -1.0, 1.0, ALU.mult, ALU.add))
                ve.wait_ge(lf_ready, h * 1 + 1)
                for n in range(TT):
                    ins = v_.tensor_tensor_scan(out=bb[:, n * P:(n + 1) * P], data0=ones[:], data1=lf[:, n * P:(n + 1) * P],
                                                initial=0.0, op0=ALU.mult, op1=ALU.add)
                ins.then_inc(b_ready, 1)
                ve.wait_ge(b_ready, h * 1 + 1)

                def differences(n):
                    l, r, m = seg(bb, LEVELS[n])
                    dl, dr, _ = seg(db[:, n % 2, :], LEVELS[n])
                    v_.tensor_tensor(dl, m, l, ALU.subtract)
                    v_.tensor_tensor(dr, r, m, ALU.subtract).then_inc(d_ready, 1)

                differences(0)
                ve.wait_ge(ek_ready, h * 1 + 1)
                evacuated(q8, j0 + 1)
                q, k = qb[:, hh, :], kb[:, hh, :]
                S.mark(v_.tensor_tensor(qoff[:, 0:2, :], q[:, P:3 * P].rearrange("p (a b) -> p a b", a=2), eq[:, P:3 * P].rearrange("p (a b) -> p a b", a=2), ALU.mult))
                S.mark(v_.tensor_tensor(qoff[:, 3, :], q[:, 3 * P:], eq[:, 3 * P:], ALU.mult))
                S.done(v_.tensor_tensor(koff[:, 0:3, :], k[:, 0:3 * P].rearrange("p (a b) -> p a b", a=3), ek[:, 0:3 * P].rearrange("p (a b) -> p a b", a=3), ALU.mult))
                v_.tensor_scalar(qoff[:, 2, :], qoff[:, 3, :], small[:, 41:42], None, ALU.mult)
                v_.tensor_scalar(koff[:, 3, :], koff[:, 0, :], small[:, 40:41], None, ALU.mult).then_inc(off_ready, 1)
                for n in range(7):
                    if n < 6:
                        if n:
                            ve.wait_ge(x_ready, h * 7 + n)
                        differences(n + 1)
                    ve.wait_ge(e_ready, h * 7 + (n + 1))
                    dl, dr, _ = seg(db[:, n % 2, :], LEVELS[n])
                    ql, qr, _ = seg(q, LEVELS[n])
                    kl, kr, _ = seg(k, LEVELS[n])
                    xl, xr, _ = seg(sq[:, n, :], LEVELS[n])
                    v_.tensor_tensor(xl, dl, kl, ALU.mult)
                    v_.tensor_tensor(xr, dr, qr, ALU.mult).then_inc(x_ready, 1)
                ve.wait_ge(v_free, h * 1 + 1)
                for n in range(8):
                    ve.wait_ge(lvl_done, h * 8 + (n + 1))
                    if n:
                        ve.wait_ge(lvl_evac, h * 8 + (n + 1))
                    bank = 7 if n % 2 == 0 else 5
                    carry_waits()
                    v_.copy_predicated(sd[:, hh], lm[:, n, :].unsqueeze(1).broadcast_to([P, TT, P]),
                                       ps[:, bank, :].rearrange("p (a b) -> p a b", a=TT)).then_inc(lvl_evac, 1)
                rsqrt_head(h)
                ve.wait_ge(o_copied, h * 1 + 2)
                S.done(v_.scalar_tensor_tensor(out=osc, in0=ob[:], scalar=cc[:, bass.ds(h * 1 + COLS["hgn"], 1)], in1=rstd[:],
                                               op0=ALU.mult, op1=ALU.mult))
                evacuated(q8, j0 + 3)
                v_.tensor_tensor(og[:, bass.ds(h, 1), :], osc.unsqueeze(1), gb[:, hh, :].unsqueeze(1), ALU.mult).then_inc(og_ready, 1)

            def rsqrt_head(h):
                rsqrt(h + RS_HEAD, P)

            with S.loop(HEADS // 2, 24) as i:
                head(i * 2, 0, i + Q_HEADS)
                head(i * 2 + 1, 1, i + Q_HEADS)

            PAD = CONV_K - 1
            S.done(v_.memset(glu[:, 0:PAD], 0.0))
            with S.loop(KT, CONV_K - 1) as i:
                q8 = i + Q_GATES
                taken(q8, 1)
                evacuated(q8, 0)
                v_.tensor_tensor(glu[:, PAD:PAD + T], ps[:, 1, :], sg[:, 0, :], ALU.mult).then_inc(bank_free[1], 1)
                ve.wait_ge(bank_free[1], q8 * 2 + 1)
                c = cv[:, bass.ds(i, 1), :]

                def tap(n):
                    return cc[:, bass.ds(i * CONV_K + (COLS["conv_w"] + n), 1)]

                S.done(v_.tensor_scalar(c, glu[:, 0:T].unsqueeze(1), tap(0), cc[:, bass.ds(i * 1 + COLS["conv_b"], 1)], ALU.mult, ALU.add))
                for n in range(1, CONV_K):
                    ins = v_.scalar_tensor_tensor(out=c, in0=glu[:, n:n + T].unsqueeze(1), scalar=tap(n), in1=c, op0=ALU.mult, op1=ALU.add)
                    if n < CONV_K - 1:
                        S.done(ins)
                    else:
                        ins.then_inc(cv_ready, 1)
                        ve.wait_ge(cv_ready, i * 1 + 1)
            ve.wait_ge(mean_done, 1)
            S.done(v_.tensor_scalar(mu[:], ps[:, 5, :], 1.0 / D, None, ALU.mult))
            for k in range(KT):
                v_.tensor_tensor(cv[:, k, :], cv[:, k, :], mu[:], ALU.subtract).then_inc(xc_ready, 1)
            for j in range(KT):
                taken(Q_WA, j)
                v_.tensor_tensor(sga[:, j, :], sga[:, j, :], ps[:, j % BANKS, :], ALU.mult).then_inc(bank_free[j % BANKS], 1)
            rsqrt(RS_LN, D)
            for k in range(KT):
                v_.scalar_tensor_tensor(out=cv[:, k, :], in0=cv[:, k, :], scalar=col("ln_g", k), in1=rstd[:],
                                        op0=ALU.mult, op1=ALU.mult).then_inc(cvn_ready, 1)
            for j in range(KT):
                taken(Q_WB, j)
                v_.tensor_tensor(sgb[:, j, :], sgb[:, j, :], ps[:, j % BANKS, :], ALU.mult).then_inc(bank_free[j % BANKS], 1)
                ve.wait_ge(bank_free[j % BANKS], 2 * Q_WB + j // BANKS + 1)
                v_.tensor_tensor(sga[:, j, :], sga[:, j, :], sgb[:, j, :], ALU.add).then_inc(m_ready, 1)

            def residual(q8, j, gain=None):
                taken(q8, j)
                if gain is not None:
                    ins = v_.scalar_tensor_tensor(out=hT[:, j, :], in0=ps[:, j % BANKS, :], scalar=ada[:, gain + j:gain + j + 1],
                                                  in1=hT[:, j, :], op0=ALU.mult, op1=ALU.add)
                else:
                    ins = v_.tensor_tensor(hT[:, j, :], ps[:, j % BANKS, :], hT[:, j, :], ALU.add)
                ins.then_inc(bank_free[j % BANKS], 1)

            for j in range(KT):
                residual(Q_WOUT, j, 16)
            gain_of(1)
            norm(1, lambda k: small[:, 32 + k:33 + k])

            def best(values_of, spare, vals, idx, first=False):
                S.done(v_.max(vals[:, 0:8], values_of))
                v_.max_index(idx[:, 0:8], vals[:, 0:8], values_of)
                S.done(v_.match_replace(spare, vals[:, 0:8], values_of, LOWEST))
                S.done(v_.max(vals[:, 8:16], spare))
                return v_.max_index(idx[:, 8:16], vals[:, 8:16], spare)

            for tt in range(TT):
                for hp in range(16):
                    if tt == 0:
                        ve.wait_ge(sc_sb, hp + 1)
                    ins = best(qpeer[:, hp, tt * P:(tt + 1) * P], srep[:], sc16[:, hp, :], ix16u[:, hp, :])
                S.done(ins)
                S.done(v_.tensor_copy(ix16[:], ix16u[:]))
                hsc = sc16.rearrange("p (h s) k -> p h s k", s=2)
                S.done(v_.tensor_tensor(cand.rearrange("p (h i j) -> p h i j", h=PEER_HEADS, i=TOPK),
                                        hsc[:, :, 0, :].unsqueeze(3).broadcast_to([P, PEER_HEADS, TOPK, TOPK]),
                                        hsc[:, :, 1, :].unsqueeze(2).broadcast_to([P, PEER_HEADS, TOPK, TOPK]), ALU.add))
                for h in range(PEER_HEADS):
                    S.mark(best(cand[:, 256 * h:256 * h + 256], crep[:], tops[:, h, :], posu[:, h * TOPK:(h + 1) * TOPK]))
                S.wait()
                S.mark(v_.tensor_scalar(piu[:, 0, :], posu[:], 4, None, ALU.logical_shift_right))
                S.done(v_.tensor_scalar(piu[:, 1, :], posu[:], 15, None, ALU.bitwise_and))
                S.done(v_.tensor_copy(pif[:], piu[:]))
                hix = ix16.rearrange("p (h s) k -> p h s k", s=2)
                for s in range(2):
                    o3 = oneh.rearrange("p (n x) -> p n x", x=TOPK)
                    S.done(v_.tensor_tensor(o3, pif[:, s, :].unsqueeze(2).broadcast_to([P, SLOTS, TOPK]),
                                            iota[:, 0:TOPK].unsqueeze(1).broadcast_to([P, SLOTS, TOPK]), ALU.is_equal))
                    o4 = oneh.rearrange("p (h n x) -> p h n x", h=PEER_HEADS, x=TOPK)
                    S.done(v_.tensor_tensor(o4, o4, hix[:, :, s, :].unsqueeze(2).broadcast_to([P, PEER_HEADS, TOPK, TOPK]), ALU.mult))
                    v_.tensor_reduce(slot[:, s, :], o3, AX.X, ALU.add).then_inc(slot_ready, 1)
                    ve.wait_ge(slot_ready, tt * 3 + (s + 1))
                g3 = slot[:, 2, :].rearrange("p (h k) -> p h k", k=TOPK)
                v_.tensor_tensor(g3, tops[:], tops[:, :, 0:1].broadcast_to([P, PEER_HEADS, TOPK]), ALU.subtract).then_inc(gate_in, 1)
                ve.wait_ge(gate_exp, tt * 1 + 1)
                S.done(v_.tensor_reduce(gsum[:, :, 0], g3, AX.X, ALU.add))
                S.done(v_.reciprocal(gsum[:, :, 1], gsum[:, :, 0]))
                v_.tensor_tensor(g3, g3, gsum[:, :, 1:2].broadcast_to([P, PEER_HEADS, TOPK]), ALU.mult).then_inc(slot_ready, 1)
                ve.wait_ge(slot_tr, tt * 1 + 1)
                if tt:
                    ve.wait_ge(hot_ready, tt * 32)
                v_.tensor_copy(slotT[:], ps[:, 4, 0:3 * P].rearrange("p (a b) -> p a b", a=3)).then_inc(slot_sb, 1)
                ve.wait_ge(slot_sb, tt * 1 + 1)
                with ve.Fori(0, 16) as i:
                    for par in range(2):
                        ve.wait_ge(gmm_done, i * 2 + (tt * 32 + par + 1))
                        for k in range(4):
                            t = i * 8 + (4 * par + k)
                            ins = v_.tensor_scalar(arng[:, 4 * par + k, :], iota[:], slotT[:, 0, bass.ds(t, 1)],
                                                   slotT[:, 2, bass.ds(t, 1)], ALU.is_equal, ALU.mult)
                            ins = v_.tensor_scalar(brng[:, 4 * par + k, :], iota[:], slotT[:, 1, bass.ds(t, 1)], None, ALU.is_equal)
                        ins.then_inc(hot_ready, 1)

            def hidden(s, q8, groups):
                def up(q, g, par):
                    for j in range(8):
                        evacuated(q, j)
                        if s == 0:
                            if j == 0:
                                ve.wait_ge(g_in[par], g * 64 + (64 if par else 128))
                            other = gi[:, par, j, :]
                        else:
                            other = gel[:, j % 4, :]
                        v_.tensor_tensor(hid[:, par, j, :], gel[:, j % 4, :], other, ALU.mult).then_inc(hid_ready[s], 1)

                def down(q):
                    for j in range(8):
                        residual(q, j, 40 if s == 0 else None)

                up(q8, 0, 0)
                with ve.Fori(0, groups // 2 - 1) as i:
                    up(i * 4 + (q8 + 1), i * 2 + 1, 1)
                    down(i * 4 + (q8 + 2))
                    up(i * 4 + (q8 + 3), i * 2 + 2, 0)
                    down(i * 4 + (q8 + 4))
                e = q8 + 2 * groups - 3
                up(e, groups - 1, 1)
                down(e + 1)
                down(e + 2)

            hidden(0, Q_PEER, 16)
            norm(2, lambda k: col("final", k))

            def attention(s, r):
                a = att[s]
                norm(r, lambda k: col("mix0" if s == 0 else "mix1", k))

                def units(n, par, hh):
                    if isinstance(n, int):
                        ve.wait_ge(strip_in[s][hh], 16 * (n + 1))
                    else:
                        ve.wait_ge(strip_in[s][hh], n * 16 + 16)
                    for qt in range(TT):
                        ve.wait_ge(a["lg_done"], n * 8 + (4 * hh + qt + 1))
                        carry_waits()
                        S.done(v_.tensor_tensor_reduce(out=pb[:, par, hh, qt, :], in0=ps[:, qt, :],
                                                       in1=strip[:, hh, P * (3 - qt):P * (3 - qt) + T], scale=1.0, scalar=LOWEST,
                                                       op0=ALU.add, op1=ALU.max, accum_out=mx[:, hh, qt:qt + 1]))
                        v_.tensor_scalar(nm[:, hh, qt:qt + 1], mx[:, hh, qt:qt + 1], -1.0, None, ALU.mult).then_inc(a["nm_ready"], 1)

                def scale_a(n, par, hh):
                    for qt in range(TT):
                        ve.wait_ge(a["p_ready"], n * 8 + (4 * hh + qt + 1))
                        S.done(v_.reciprocal(rz[:, hh, qt:qt + 1], zt[:, hh, qt:qt + 1]))
                        v_.tensor_scalar(pb[:, par, hh, qt, :], pb[:, par, hh, qt, :], rz[:, hh, qt:qt + 1], None,
                                         ALU.mult).then_inc(a["pn_ready"], 1)
                    h = n * 2 + hh
                    sl = slice(h, h + 1) if isinstance(h, int) else bass.ds(h, 1)
                    v_.tensor_copy(zs[:, 0, sl, :], mx[:, hh, :].unsqueeze(1))
                    S.mark(v_.tensor_copy(zs[:, 1, sl, :], zt[:, hh, :].unsqueeze(1)))

                def combine_b(n, par):
                    for qt in range(TT):
                        ve.wait_ge(a["p_ready"], n * 8 + (4 + qt + 1))
                        S.mark(v_.reciprocal(rz[:, 0, qt:qt + 1], zt[:, 0, qt:qt + 1]))
                        S.done(v_.reciprocal(rz[:, 1, qt:qt + 1], zt[:, 1, qt:qt + 1]))
                        S.mark(v_.tensor_scalar(pb[:, par, 0, qt, :], pb[:, par, 0, qt, :], rz[:, 0, qt:qt + 1], None, ALU.mult))
                        S.done(v_.tensor_scalar(rz[:, 1, qt:qt + 1], rz[:, 1, qt:qt + 1], lamc[:, 3:4], None, ALU.mult))
                        v_.scalar_tensor_tensor(out=pb[:, par, 0, qt, :], in0=pb[:, par, 1, qt, :], scalar=rz[:, 1, qt:qt + 1],
                                                in1=pb[:, par, 0, qt, :], op0=ALU.mult, op1=ALU.add).then_inc(a["pn_ready"], 1)

                def out_b(u, par):
                    rsqrt(u + RS_B, P, 7)
                    dst = uT[:, u:u + 1, :] if isinstance(u, int) else uT[:, bass.ds(u, 1), :]
                    v_.scalar_tensor_tensor(out=dst, in0=sq[:, 1 + par, :].unsqueeze(1), scalar=subc[:, 0:1], in1=rstd[:].unsqueeze(1),
                                            op0=ALU.mult, op1=ALU.mult).then_inc(a["oT_ready"], 1)

                if s == 0:
                    with S.loop(4, 4 * 9) as i:
                        for par in range(2):
                            for hh in range(2):
                                units(i * 2 + par, par, hh)
                                scale_a(i * 2 + par, par, hh)
                    S.wait()
                    v_.engine_nop() if False else None
                    v_.tensor_copy(gm[:, 3, :], gm0[:]).then_inc(a["lse"], 1)
                    ve.wait_ge(a["lse"], 2)
                    S.done(v_.tensor_tensor(zs[:, 0], zs[:, 0], zs[:, 2], ALU.add))
                    S.done(v_.tensor_reduce(gm[:, 0, :], zs[:, 0].rearrange("p h q -> p q h"), AX.X, ALU.max))
                    v_.tensor_tensor(zs[:, 0], zs[:, 0], gm[:, 0, :].unsqueeze(1).broadcast_to([P, A_HEADS, TT]), ALU.subtract).then_inc(a["lse"], 1)
                    ve.wait_ge(a["lse"], 4)
                    h0 = 0
                    for g, (_, _, nh) in enumerate(A_GROUPS):
                        S.done(v_.tensor_reduce(wg[:, g, :], zs[:, 1, h0:h0 + nh, :].rearrange("p h q -> p q h"), AX.X, ALU.add))
                        S.done(v_.tensor_scalar(wg[:, g, :], wg[:, g, :], 1.0 / nh, None, ALU.mult))
                        h0 += nh
                    S.done(v_.tensor_tensor(gm[:, 1, :], wg[:, 0, :], wg[:, 1, :], ALU.add))
                    S.done(v_.tensor_tensor(gm[:, 1, :], gm[:, 1, :], wg[:, 2, :], ALU.add))
                    S.done(v_.reciprocal(gm[:, 2, :], gm[:, 1, :]))
                    S.done(v_.tensor_scalar(gm[:, 2, :], gm[:, 2, :], float(len(A_GROUPS)), None, ALU.mult))
                    v_.tensor_tensor(wg[:], wg[:], gm[:, 2, :].unsqueeze(1).broadcast_to([P, 3, TT]), ALU.mult).then_inc(al_ready, 1)
                    ve.wait_ge(alb_sb, 3)
                    ve.wait_ge(a["o_ready"], 18)
                    h = 0
                    for g, (_, _, nh) in enumerate(A_GROUPS):
                        for _ in range(nh):
                            rows = slice(64 * (h % 2), 64 * (h % 2) + 64)
                            v_.tensor_tensor(uT[rows, h // 2, :], uT[rows, h // 2, :], alb[rows, g, :], ALU.mult).then_inc(a["oT_ready"], 1)
                            h += 1
                else:
                    units(0, 0, 0)
                    units(0, 0, 1)
                    combine_b(0, 0)
                    with S.loop(3, 58) as i:
                        units(i * 2 + 1, 1, 0)
                        units(i * 2 + 1, 1, 1)
                        combine_b(i * 2 + 1, 1)
                        out_b(i * 2, 0)
                        units(i * 2 + 2, 0, 0)
                        units(i * 2 + 2, 0, 1)
                        combine_b(i * 2 + 2, 0)
                        out_b(i * 2 + 1, 1)
                    units(7, 1, 0)
                    units(7, 1, 1)
                    combine_b(7, 1)
                    out_b(6, 0)
                    out_b(7, 1)

            S.done(v_.memset(gm0[:], 0.0))
            attention(0, 3)
            for j in range(KT):
                residual(Q_WO_A, j)
            norm(4, lambda k: col("mlp0", k))
            hidden(1, Q_MLP_A, 4)
            ve.wait_ge(lb_sem, 4)
            S.done(v_.tensor_tensor(lamc[:, 2:3], lamc[:, 1:2], lamc[:, 0:1], ALU.subtract))
            S.done(v_.tensor_scalar(lamc[:, 3:4], lamc[:, 2:3], -LAMBDA_INIT, None, ALU.add))
            attention(1, 5)
            for j in range(KT):
                residual(Q_WO_B, j)
            norm(6, lambda k: col("mlp1", k))
            hidden(2, Q_MLP_B, 4)
            norm(7, lambda k: col("final2", k))

        @block.gpsimd
        def _(po):
            for s in (v_free, gmm_done, g_evac, att[0]["pt_ready"], att[1]["pt_ready"], att[0]["o_ready"]):
                po.sem_inc(s, 2)
            for s in (f_ready, og_ready, lvl_evac, o_copied, att[1]["o_ready"]):
                po.sem_inc(s, 1)
            po.sem_inc(g_out, 16)
            def stage(s, n, par, used):
                if used is not None:
                    po.wait_ge(att[s]["av_done"], used)
                sl = slice(n, n + 1) if isinstance(n, int) else bass.ds(n, 1)
                g_.tensor_copy(qs[:, par:par + 1, :], qT[:, sl, :]).then_inc(att[s]["staged"], 1)
                g_.tensor_copy(ks[:, par:par + 1, :], kT[:, sl, :]).then_inc(att[s]["staged"], 1)
                vsl = slice(n * P, n * P + P) if isinstance(n, int) else bass.ds(n * P, P)
                g_.tensor_copy(vs[:, par], vtok[:, :, vsl]).then_inc(att[s]["staged"], 1)

            for s, q in ((0, Q_QKV_A), (1, Q_QKV_B)):
                for b in range(BANKS):
                    po.wait_ge(bank_free[b], 2 * (q + 3))
                stage(s, 0, 0, None)
                stage(s, 1, 1, None)
                with po.Fori(0, 3) as i:
                    for par in range(2):
                        stage(s, i * 2 + (2 + par), par, i * 4 + (2 + 2 * par) if s == 0 else i * 2 + (1 + par))


def lay_out(inputs):
    f = {k: np.asarray(v) for k, v in inputs.items()}

    def pan(w):
        K, N = w.shape
        return w.reshape(K // D, KT, P, N // P, P).transpose(0, 3, 2, 1, 4)

    def hidden(up, down, groups):
        up = up.reshape(groups, 8, P, KT, P)
        out = [up[0]]
        for g in range(groups):
            if g + 1 < groups:
                out.append(up[g + 1])
            out.append(down[g])
        return out

    ada = pan(f["ada_w"][0])[0]
    z = pan(f["w_in"][0])[0].reshape(8, 8, P, KT, P)
    zq, zf, zi, zg, zca, zcb, zga, zgb = z
    seq = [ada[0:16]]
    seq.append(np.stack([zf, zq, zi, zg], 1).reshape(32, P, KT, P))
    rest = ada[16:48].reshape(8, 4, P, KT, P)
    seq.append(np.stack([zcb, zca, rest[:, 0], zga, rest[:, 1], zgb, rest[:, 2], rest[:, 3]], 1).reshape(64, P, KT, P))
    seq += [pan(f["w_a"][0])[0], pan(f["w_b"][0])[0], pan(f["w_out"][0])[0], pan(f["peer_wq"][0])[0]]
    up = f["peer_u"][0].reshape(NKEYS, P, KT, P).transpose(0, 3, 2, 1)
    seq += hidden(up, pan(f["peer_v"][0]), 16)
    for s, (qkv, wo) in enumerate((("a_w_qkv_2", "a_w_o_2"), ("b_w_qkv_2", "b_w_o_2"))):
        seq += [pan(f[qkv][0])[0], pan(f[wo][0])[0]]
        seq += hidden(pan(f["mlp_w_in_2"][s])[0], pan(f["mlp_w_out_2"][s]), 4)
    panels = np.concatenate(seq, 0)
    assert panels.shape[0] == 8 * Q_END

    def c(a):
        return np.asarray(a).reshape(-1, P).T

    conv = f["conv_w"][0].reshape(CONV_K, KT, P).transpose(2, 1, 0).reshape(P, KT * CONV_K)
    cols = np.concatenate([
        c(f["c"]), c(f["ada_b"]), c(f["norm1_g"]), c(f["lb_logits"][0]), c(f["lb_logits"][1]), c(f["hg_norm_g"]), conv,
        c(f["conv_b"]), c(f["conv_ln_g"]), c(f["conv_ln_b"]), c(f["norm2_g"]), c(f["final_g"]),
        c(f["norm_mix_g_2"][0]), c(f["norm_mix_g_2"][1]), c(f["norm_mlp_g_2"][0]), c(f["norm_mlp_g_2"][1]),
        c(f["norm_final_g_2"]), c(f["b_subln_g_2"])], 1)
    consts = np.concatenate([np.eye(P, dtype=np.float32), np.tile(np.arange(P, dtype=np.float32), (P, 1))], 1)
    s_, t_ = np.arange(P)[:, None], np.arange(P)[None, :]
    masks = [((s_ // (2 * L) == t_ // (2 * L)) & (s_ % (2 * L) < L) & (t_ % (2 * L) >= L)) for L in LEVELS] + [s_ == t_]
    lmask = np.stack(masks, 1).astype(np.uint32)
    keysT = f["peer_keys"][0].reshape(16, NKEYS, P).transpose(2, 0, 1)
    rel = np.arange(1024) - 511
    n = np.abs(rel)
    nf = np.maximum(n, 1).astype(np.float32)
    large = 8 + (np.log(nf / np.float32(8)) / np.float32(np.log(1024 / 8)) * np.float32(8)).astype(np.int32)
    bucket = np.where(rel > 0, 16, 0) + np.where(n < 8, n, np.minimum(large, 15))
    oh = np.zeros((35, 2, 1024), np.float32)
    oh[:32] = (bucket[None, :] == np.arange(32)[:, None])[:, None, :]
    member = np.zeros((3, A_HEADS), np.float32)
    h0 = 0
    for g, (win, dil, nh) in enumerate(A_GROUPS):
        side = win // (2 * dil)
        oh[32 + g, 0] = np.where((n <= side * dil) & (n % dil == 0), 0.0, NEG)
        member[g, h0:h0 + nh] = 1.0
        h0 += nh
    return {
        "panels": panels, "xT": f["x"][0].T.reshape(KT, P, T).transpose(1, 0, 2), "cols": cols, "consts": consts,
        "lmask": lmask, "keysT": keysT, "oh": oh, "rel": np.concatenate([f["rel_bias_2"], member], 0),
        "blam": np.broadcast_to(f["b_lambda_2"].reshape(1, 4, 64), (P, 4, 64)),
    }


def kernel(**inputs):
    import concourse.bacc as bacc
    from concourse.bass_utils import run_bass_kernel_spmd

    nc = bacc.Bacc("TRN2", target_bir_lowering=False, num_devices=1)
    arrays, args = {}, []
    for name, a in lay_out(inputs).items():
        arrays[name] = np.ascontiguousarray(a)
        args.append(nc.dram_tensor(name, a.shape, mybir.dt.from_np(a.dtype), kind="ExternalInput").ap())
    F32 = mybir.dt.float32
    outT = nc.dram_tensor("outT", [P, KT, T], F32, kind="ExternalOutput").ap()
    gdram = nc.dram_tensor("gdram", [TT, NKEYS, P, P], F32, kind="Internal").ap()
    btab = nc.dram_tensor("btab", [2, A_HEADS, 1024], F32, kind="Internal").ap()
    strips_dram = nc.dram_tensor("strips_dram", [2 * A_HEADS, P, STRIP], F32, kind="Internal").ap()
    build(nc, *args, outT, gdram, btab, strips_dram)
    r = run_bass_kernel_spmd(nc, [arrays], core_ids=[0])
    y = r.results[0]["outT"]
    return np.ascontiguousarray(np.asarray(y).transpose(2, 1, 0).reshape(1, T, D))
```

```python
from contextlib import ExitStack, contextmanager

import numpy as np

import concourse.bass as bass
from concourse import mybir
from concourse.alu_op_type import AluOpType as ALU

P = 128
T = 512
D = 1024
KT = D // P
TT = T // P
EPS = 1e-6
HEADS = 8
CONV_K = 31
LEVELS = (64, 32, 16, 8, 4, 2, 1)
PEER_HEADS, NKEYS, TOPK = 8, 128, 16
SLOTS = PEER_HEADS * TOPK
A_HEADS = 16
A_GROUPS = ((128, 1, 6), (512, 4, 5), (2048, 16, 5))
B_HEADS = 8
EARLY = 10
LAMBDA_INIT = 0.8 - 0.6 * float(np.exp(-0.3))
NEG = -1.0e30
LOWEST = -3.0e38
STRIP = T + (TT - 1) * P
RING = 4
BANKS = 4

Q_ADA1, Q_HEADS, Q_GATES, Q_WA, Q_WB, Q_WOUT, Q_WQ, Q_PEER = 0, 2, 6, 14, 15, 16, 17, 19
Q_QKV_A, Q_WO_A, Q_MLP_A = 51, 54, 55
Q_QKV_B, Q_WO_B, Q_MLP_B, Q_END = 63, 66, 67, 75
WHOLE = 8 * (Q_WA - Q_GATES)
N_SPLIT = 8 * (Q_END - Q_HEADS) - WHOLE

COLS = {}
_n = 0
for _name, _w in (("c", 8), ("ada_b", 48), ("norm1", 8), ("lb0", 8), ("lb1", 8), ("hgn", 8), ("conv_w", 8 * CONV_K),
                  ("conv_b", 8), ("ln_g", 8), ("ln_b", 8), ("norm2", 8), ("final", 8), ("mix0", 8), ("mix1", 8),
                  ("mlp0", 8), ("mlp1", 8), ("final2", 8), ("subln", 1)):
    COLS[_name] = _n
    _n += _w
NCOLS = _n
RS_NORM = (0, 10, 11, 12, 13, 14, 23, 24)
RS_HEAD, RS_LN, RS_B = 1, 9, 15
SPLIT_NORM = {0: 0, 1: 1, 3: 2, 4: 3, 5: 4, 6: 5}


class Steps:

    def __init__(self, eng, sem):
        self.eng, self.sem, self.count, self.regs = eng, sem, 0, []

    def value(self):
        v = self.count
        for reg, per in self.regs:
            v = reg * per + v
        return v

    def mark(self, ins):
        ins.then_inc(self.sem, 1)
        self.count += 1

    def wait(self):
        self.eng.wait_ge(self.sem, self.value())

    def done(self, ins):
        self.mark(ins)
        self.wait()

    @contextmanager
    def loop(self, n, per):
        at = self.count
        with self.eng.Fori(0, n) as i:
            self.regs.append((i, per))
            yield i
            self.regs.pop()
        assert self.count - at == per, (self.count - at, per)
        self.count = at + n * per


def build(nc, panels, xT, cols, consts, lmask, keysT, oh, rel, blam, outT, gdram, adram, btab, strips_dram):
    F32 = mybir.dt.float32
    U32 = mybir.dt.uint32
    ACT = mybir.ActivationFunctionType
    AX = mybir.AxisListType
    v_, s_, g_, t_ = nc.vector, nc.scalar, nc.gpsimd, nc.tensor
    ctx = ExitStack()
    with ctx:
        def sb(name, shape, dt=F32):
            return ctx.enter_context(nc.sbuf_tensor(name, shape, dt))

        F32R = mybir.dt.float32r

        def both(name, shape):
            with nc.sbuf_tensor(name, shape, F32) as t:
                pass
            return t, ctx.enter_context(nc.sbuf_tensor(name + "_r", shape, F32R))

        def sem(name):
            return ctx.enter_context(nc.semaphore(name))

        ps = ctx.enter_context(nc.psum_tensor("ps", [P, 8, 512], F32))
        hT = sb("hT", [P, KT, T])
        BF16 = mybir.dt.bfloat16
        uT, uT_r = both("uT", [P, KT, T])
        ring, ring_r = both("ring", [P, RING, KT, P])
        high_w = sb("high_w", [P, RING, KT, P], F32R)
        sq, sq_r = both("sq", [P, KT, T])
        st = sb("st", [P, 4, T])
        ms, sr, rt, rstd = (st[:, n, :] for n in range(4))
        cc = sb("cc", [P, NCOLS])
        cst = sb("cst", [P, 2 * P])
        ones = sb("ones", [P, P])
        act_out = sb("act_out", [P, 1, T])
        rbs = sb("rbs", [35, 16])
        ada = sb("ada", [P, 48])
        small = sb("small", [P, 96])
        with nc.sbuf_tensor("arena", [P, 27520], F32) as arena:
            pass
        parts = [sb(f"part{n}", [P, KT, T], F32R) for n in range(4)]
        sb("between", [P, 20000 - 4 * KT * T])
        part_x = sb("part_x", [P, KT, T], F32R)
        sb("rest", [P, 27520 - 20000 - KT * T])
        ident, iota = cst[:, 0:P], cst[:, P:2 * P]

        def view(at, *shape):
            n = int(np.prod(shape))
            a = arena[:, at:at + n]
            if len(shape) == 1:
                return a
            names = "abcd"[:len(shape)]
            return a.rearrange("p (" + " ".join(names) + ") -> p " + " ".join(names),
                               **{names[k]: shape[k] for k in range(1, len(shape))})


        og, cv, sga, sgb = (view(4096 * n, KT, T) for n in range(4))
        og_r, cv_r, sga_r = parts[:3]
        at = 4096
        ohs = arena[0:35, 20000:22048].rearrange("p (a b) -> p a b", a=2)
        gtab = arena[0:16, 23000:25048].rearrange("p (a b) -> p a b", a=2)
        lm = arena[:, 18944:19968].bitcast(U32).rearrange("p (a b) -> p a b", a=8)
        osc = view(25100, T)
        ulo = part_x
        cvh = part_x
        lam = view(25700, 4, 64)
        lamt = view(25956, 64)
        qb = view(at, 2, T)
        kb = view(at + 1024, 2, T)
        vb = view(at + 2048, 2, TT, P)
        gb = view(at + 3072, 2, T)
        eb = view(at + 4096, T)
        fb = view(at + 4608, T)
        lf = view(at + 5120, T)
        bb = view(at + 5632, T)
        eq = view(at + 6144, T)
        ek = view(at + 6656, T)
        qoff = view(at + 7168, 4, P)
        koff = view(at + 7680, 4, P)
        db = view(at + 8192, 2, T)
        sd = view(at + 9216, 2, TT, P)
        soff = view(at + 10240, 2, 6, P)
        ob = view(at + 11776, T)
        osq = view(at + 12288, T)
        sg = view(16384, 2, T)
        glu = view(16384 + 1024, T + 32)
        mu = view(16384 + 2048, T)
        qpeer = view(0, 16, T)
        gbuf = view(8192, NKEYS, P)
        ky = view(8192, 16, P)
        srep = view(26624, P)
        arng = st[:, 0:2, :].rearrange("p a (b c) -> p (a b) c", c=P)
        brng = st[:, 2:4, :].rearrange("p a (b c) -> p (a b) c", c=P)
        tk = 26752
        sc16, ix16 = view(tk, 16, TOPK), view(tk + 512, 16, TOPK)
        ix16u = arena[:, tk + 256:tk + 512].bitcast(U32).rearrange("p (a b) -> p a b", b=TOPK)
        cand = view(24576, 2048)
        oneh = cand
        tops = sb("tops", [P, PEER_HEADS, TOPK])
        posu = sb("posu", [P, SLOTS], U32)
        piu = sb("piu", [P, 2, SLOTS], U32)
        pif = piu[:].rearrange("p a b -> p (a b)").bitcast(F32).rearrange("p (a b) -> p a b", a=2)
        slot = sb("slot", [P, 3, SLOTS])
        slotT = sb("slotT", [P, 3, P])
        gsum = sb("gsum", [P, PEER_HEADS, 2])
        crep = slotT[:].rearrange("p a b -> p (a b)")[:, 0:256]
        hid = [parts[2 * par:2 * par + 2] for par in range(2)]
        gel = view(16384, 4, T)
        gi = view(18432, 2, KT, T)
        qT, kT = (view(4096 * n, KT, T) for n in range(2))
        qT_r = parts[0]
        vtok = view(8192, TT, D)
        pb = view(12288, 2, 2, TT, T)
        strip = view(20480, 2, STRIP)
        pt = view(22272, 2, TT, T)
        qs = sq[:, 3:5, :]
        ks = sq[:, 5:7, :]
        vf = view(22272, 2, T)
        vs = view(26368, 2, TT, P)
        zs = slot[:, :, 0:A_HEADS * TT].rearrange("p a (b c) -> p a b c", c=TT)
        wg = sb("wg", [P, 3, TT])
        gm = sb("gm", [P, 4, TT])
        nm = sb("nm", [P, 2, TT])
        rz = sb("rz", [P, 2, TT])
        mx = sb("mx", [P, 2, TT])
        zt = sb("zt", [P, 2, TT])
        lbt = sb("lbt", [P, 24])
        lamc = sb("lamc", [P, 4])
        subc = sb("subc", [P, 1])
        alb = view(12288, 3, T)

        w_slot = [sem(f"w_slot{i}") for i in range(RING)]
        hi_ready, lo_ready = sem("hi_ready"), sem("lo_ready")
        gemm_done = sem("gemm_done")
        bank_free = [sem(f"bank_free{i}") for i in range(BANKS)]
        x_in, c_in, in_ready = sem("x_in"), sem("c_in"), sem("in_ready")
        dve_step, ones_set = sem("dve_step"), sem("ones_set")
        sq_ready, u_ready = sem("sq_ready"), sem("u_ready")
        stat_done, rs_ms, rs_sqrt = sem("stat_done"), sem("rs_ms"), sem("rs_sqrt")
        silu_c = sem("silu_c")
        strips_out = sem("strips_out")
        tab_done, tab_sb, tab_dram = sem("tab_done"), sem("tab_sb"), sem("tab_dram")
        lb_sem = sem("lb_sem")
        f_ready, lf_ready, b_ready, ek_ready = sem("f_ready"), sem("lf_ready"), sem("b_ready"), sem("ek_ready")
        off_ready, off_done, soff_ready = sem("off_ready"), sem("off_done"), sem("soff_ready")
        d_ready, e_ready, x_ready = sem("d_ready"), sem("e_ready"), sem("x_ready")
        lvl_done, lvl_evac, v_free = sem("lvl_done"), sem("lvl_evac"), sem("v_free")
        o_copied, osq_ready, og_ready = sem("o_copied"), sem("osq_ready"), sem("og_ready")
        cv_ready, mean_done, xc_ready, cvn_ready, cvs_ready = (sem(n) for n in (
            "cv_ready", "mean_done", "xc_ready", "cvn_ready", "cvs_ready"))
        m_ready, lnsq_ready, upre = sem("m_ready"), sem("lnsq_ready"), sem("upre")
        shifted, x_high, warm = sem("shifted"), sem("x_high"), sem("warm")
        sc_done, sc_sb, ky_in = sem("sc_done"), sem("sc_sb"), sem("ky_in")
        gate_in, gate_exp, slot_ready, slot_tr, slot_sb = (sem(n) for n in (
            "gate_in", "gate_exp", "slot_ready", "slot_tr", "slot_sb"))
        hot_ready, gmm_done, g_evac, g_out = (sem(n) for n in (
            "hot_ready", "gmm_done", "g_evac", "g_out"))
        a_out = sem("a_out")
        a_in = [sem(f"a_in{i}") for i in range(4)]
        vt_done, vt_sb = sem("vt_done"), sem("vt_sb")
        g_in = [sem(f"g_in{i}") for i in range(2)]
        hid_ready = [sem(f"hid_ready{i}") for i in range(3)]
        strip_in = [[sem(f"strip_in{s}{i}") for i in range(2)] for s in range(2)]
        att = []
        for s in range(2):
            att.append({n: sem(f"{n}_{s}") for n in (
                "staged", "lg_done", "nm_ready", "p_ready", "pn_ready", "tr_done", "pt_ready", "av_done",
                "o_ready", "oT_ready", "lse")})
        al_ready, alb_done, alb_sb = sem("al_ready"), sem("alb_done"), sem("alb_sb")
        bsq_ready = sem("bsq_ready")
        out_done, carried = sem("out_done"), sem("carried")

        block = ctx.enter_context(nc.Block())

        def col(name, k=0):
            return cc[:, COLS[name] + k:COLS[name] + k + 1]

        @block.sync
        def _(sp):
            for j in range(RING):
                sp.dma_start(ring[:, j], panels[j]).then_inc(w_slot[j], 16)
            with sp.Fori(0, 8 * Q_END // RING - 1) as i:
                for j in range(RING):
                    sp.wait_ge(gemm_done, i * RING + (j + 1))
                    sp.dma_start(ring[:, j], panels[i * RING + (RING + j)]).then_inc(w_slot[j], 16)
            sp.wait_ge(u_ready, 72)
            sp.dma_start(outT, sq[:]).then_inc(out_done, 16)
            sp.wait_ge(out_done, 16)

        @block.tensor
        def _(pe):
            not_split = [8 * Q_HEADS]

            def start_panel(q8, j, split, unit=8):
                if unit == 4:
                    pe.wait_ge(lo_ready, q8 * 4 + (j + 1 - not_split[0]))
                    pe.wait_ge(bank_free[j], q8 * 1 + 0)
                    return
                if split:
                    pe.wait_ge(lo_ready, q8 * 8 + (j + 1 - not_split[0]))
                else:
                    pe.wait_ge(w_slot[j % RING], q8 * 32 + 16 * (j // RING + 1))
                if not (isinstance(q8, int) and q8 * 2 + j // BANKS == 0):
                    pe.wait_ge(bank_free[j % BANKS], q8 * 2 + j // BANKS)

            def panel(q8, j, x, n=T, unit=8, ready=None):
                split = isinstance(x, tuple)
                start_panel(q8, j, split, unit)
                out = ps[:, j % BANKS, 0:n]
                for k in range(KT):
                    if ready:
                        pe.wait_ge(ready[0], ready[1] + k + 1)
                    if split:
                        wh, wl = (w[:, j % RING, k, :] for w in (high_w, ring_r))
                        xh, xl = (part[:, k, :] for part in x)
                        t_.matmul(out, wh, xh, start=(k == 0), stop=False)
                        t_.matmul(out, wh, xl, start=False, stop=False)
                        last = t_.matmul(out, wl, xh, start=False, stop=(k == KT - 1))
                    else:
                        last = t_.matmul(out, ring[:, j % RING, k, :], x[:, k, 0:n], start=(k == 0), stop=(k == KT - 1))
                last.then_inc(gemm_done, 1)

            def panel_tok(q8, j, x):
                start_panel(q8, j, True)
                for tt in range(TT):
                    out = ps[:, j % BANKS, tt * P:(tt + 1) * P]
                    for k in range(KT):
                        wh, wl = (w[:, j % RING, k, :] for w in (high_w, ring_r))
                        xh, xl = (part[:, k, tt * P:(tt + 1) * P] for part in x)
                        t_.matmul(out, xh, wh, start=(k == 0), stop=False)
                        t_.matmul(out, xl, wh, start=False, stop=False)
                        last = t_.matmul(out, xh, wl, start=False, stop=(k == KT - 1))
                last.then_inc(gemm_done, 1)

            def stat(idx, tiles, ready, at):
                if idx:
                    pe.wait_ge(rs_ms, idx)
                for k, tile in enumerate(tiles):
                    pe.wait_ge(ready, at + k + 1)
                    last = t_.matmul(ps[:, 4, :], ones[:], tile, start=(k == 0), stop=(k == len(tiles) - 1))
                last.then_inc(stat_done, 1)

            def normed(r):
                return u_ready, KT * (r + (1 if r else 0))

            def square_sum(r, k):
                if k == 0 and r:
                    pe.wait_ge(rs_ms, RS_NORM[r])
                pe.wait_ge(sq_ready, KT * r + k + 1)
                ins = t_.matmul(ps[:, 4, :], ones[:], sq[:, k, :], start=(k == 0), stop=(k == KT - 1))
                if k == KT - 1:
                    ins.then_inc(stat_done, 1)

            def behind(r, j):
                if j >= 2:
                    square_sum(r, j - 2)

            def norm(r):
                for k in range(0 if r in (0, 3) else KT - 2, KT):
                    square_sum(r, k)

            pe.wait_ge(c_in, 16 * 6)
            for tab in range(2):
                for half in range(2):
                    last = t_.matmul(ps[0:16, 4 + 2 * tab + half, :], rbs[:], ohs[:, tab, half * 512:half * 512 + 512],
                                     start=True, stop=True)
            last.then_inc(tab_done, 1)
            pe.wait_ge(tab_sb, 1)
            pe.wait_ge(ones_set, 1)
            stat(0, [sq[:, k, :] for k in range(KT)], sq_ready, 0)
            pe.wait_ge(silu_c, 1)
            cvec = small[:, 0:8].unsqueeze(2)
            for j in range(16):
                panel(j // 8, j % 8, cvec, 1)
            pe.wait_ge(tab_sb, 4)

            def head_off(h):
                pe.wait_ge(lvl_evac, h * 8 + 1)
                pe.wait_ge(o_copied, h * 1 + 1)
                pe.wait_ge(off_ready, h * 1 + 1)
                t_.matmul(ps[:, 5, 0:P], koff[:, 0, :], qoff[:, 0, :], start=True, stop=True)
                t_.matmul(ps[:, 5, P:2 * P], koff[:, 2, :], qoff[:, 3, :], start=True, stop=True).then_inc(off_done, 1)
                t_.matmul(ps[:, 6, 0:2 * P], koff[:, 3, :], qoff[:, 1:3, :], start=True, stop=True)
                t_.matmul(ps[:, 6, 2 * P:4 * P], koff[:, 1, :], qoff[:, 1:3, :], start=True, stop=True).then_inc(off_done, 1)

            def head_level(h, hh, n):
                bank = 7 if n % 2 == 0 else 5
                if n == 1:
                    pe.wait_ge(soff_ready, h * 2 + 1)
                elif n >= 2:
                    pe.wait_ge(lvl_evac, h * 8 + n)
                if n < 7:
                    pe.wait_ge(x_ready, h * 7 + (n + 1))
                for tt in range(TT):
                    if n < 7:
                        a = b = sq[:, n, tt * P:(tt + 1) * P]
                    else:
                        a, b = kb[:, hh, tt * P:(tt + 1) * P], qb[:, hh, tt * P:(tt + 1) * P]
                    last = t_.matmul(ps[:, bank, tt * P:(tt + 1) * P], a, b, start=True, stop=True)
                last.then_inc(lvl_done, 1)

            PAIRS = {(0, 1): 0, (2, 3): 1, (0, 2): 2, (0, 3): 3, (1, 2): 4, (1, 3): 5}

            def head_pv(h, hh):
                pe.wait_ge(soff_ready, h * 2 + 2)
                pe.wait_ge(lvl_evac, h * 8 + 9)
                for j in range(TT):
                    for i in range(j + 1):
                        S = sd[:, hh, j, :] if i == j else soff[:, hh, PAIRS[i, j], :]
                        last = t_.matmul(ps[:, 6, j * P:(j + 1) * P], vb[:, hh, i, :], S, start=(i == 0), stop=(i == j))
                last.then_inc(v_free, 1)

            def head_stat(h):
                pe.wait_ge(rs_ms, h * 1 + RS_HEAD)
                pe.wait_ge(osq_ready, h * 1 + 1)
                t_.matmul(ps[:, 4, :], ones[:], osq[:], start=True, stop=True).then_inc(stat_done, 1)

            def head_gemm(q8, j0, n, ready=None):
                if n == 2:
                    panel_tok(q8, j0 + 2, (uT_r, ulo))
                else:
                    panel(q8, j0 + n, (uT_r, ulo), ready=ready)

            def head_step(h, hh, q8n, jn, nxt=True, before=True):
                if nxt:
                    head_gemm(q8n, jn, 0)
                    head_gemm(q8n, jn, 1)
                head_off(h)
                head_level(h, hh, 0)
                if before:
                    head_stat(h - 1 if isinstance(h, int) else h + (-1))
                head_level(h, hh, 1)
                if nxt:
                    head_gemm(q8n, jn, 2)
                for n in (2, 3, 4):
                    head_level(h, hh, n)
                if nxt:
                    head_gemm(q8n, jn, 3)
                for n in (5, 6, 7):
                    head_level(h, hh, n)
                head_pv(h, hh)

            for n in range(4):
                head_gemm(Q_HEADS, 0, n, None if n else normed(0))
            head_step(0, 0, Q_HEADS, 4, before=False)
            with pe.Fori(0, HEADS // 2 - 1) as i:
                head_step(i * 2 + 1, 1, i + (Q_HEADS + 1), 0)
                head_step(i * 2 + 2, 0, i + (Q_HEADS + 1), 4)
            def gates_panel(q8, j):
                if j in (0, 1, 3, 5):
                    panel(q8, j, uT)
                else:
                    panel(q8, j, cvec, 1)

            head_off(7)
            head_level(7, 1, 0)
            head_stat(6)
            head_level(7, 1, 1)
            pe.wait_ge(u_ready, 2 * KT)
            gates_panel(Q_GATES, 0)
            for n in (2, 3, 4):
                head_level(7, 1, n)
            gates_panel(Q_GATES, 1)
            for n in (5, 6, 7):
                head_level(7, 1, n)
            head_pv(7, 1)
            gates_panel(Q_GATES, 2)
            gates_panel(Q_GATES, 3)
            head_stat(7)
            not_split[0] += WHOLE
            with pe.Fori(0, KT - 1) as i:
                for j in range(4, 8):
                    gates_panel(i + Q_GATES, j)
                for j in range(4):
                    gates_panel(i + (Q_GATES + 1), j)
            for j in range(4, 8):
                gates_panel(Q_GATES + KT - 1, j)
            for k in range(KT):
                pe.wait_ge(cv_ready, k + 1)
                last = t_.matmul(ps[:, 5, :], ones[:], cv[:, k, :], start=(k == 0), stop=(k == KT - 1))
            last.then_inc(mean_done, 1)
            for j in range(KT):
                if j == 4:
                    stat(RS_LN, [sq[:, k, :] for k in range(KT)], lnsq_ready, 0)
                panel(Q_WA, j, (uT_r, og_r), ready=None if j else (in_ready, 0))
            for j in range(KT):
                panel(Q_WB, j, (cvh, cv_r), ready=None if j else (in_ready, KT))
            for j in range(KT):
                panel(Q_WOUT, j, (uT_r, sga_r), ready=None if j else (m_ready, 0))
                behind(1, j)
            norm(1)

            for j in range(16):
                panel(Q_WQ + j // 8, j % 8, (uT_r, sq_r), ready=None if j else normed(1))
            for b in range(BANKS):
                pe.wait_ge(bank_free[b], 2 * (Q_WQ + 2))
            pe.wait_ge(ky_in, 16)
            for hp in range(16):
                if hp >= 4:
                    pe.wait_ge(sc_sb, hp - 3)
                for tt in range(TT):
                    last = t_.matmul(ps[:, hp % 4, tt * P:(tt + 1) * P], qpeer[:, hp, tt * P:(tt + 1) * P], ky[:, hp, :],
                                     start=True, stop=True)
                last.then_inc(sc_done, 1)
            pe.wait_ge(sc_sb, 16)
            for tt in range(TT):
                with pe.Fori(0, 3) as i:
                    for j in range(4):
                        panel(i + (2 * Q_PEER + 4 * tt), j, (uT_r, sq_r), unit=4)
                pe.wait_ge(slot_ready, 3 * (tt + 1))
                for n in range(3):
                    last = t_.transpose(ps[:, 4, n * P:(n + 1) * P], slot[:, n, :], ident)
                last.then_inc(slot_tr, 1)
                for c in range(4):
                    with pe.Fori(0, 4) as i:
                        for par in range(2):
                            n = i * 2 + (tt * 32 + 8 * c + par)
                            pe.wait_ge(hot_ready, n * 1 + 1)
                            pe.wait_ge(g_evac, n * 1 + 1)
                            for k in range(4):
                                last = t_.matmul(ps[:, 6 + par, k * P:(k + 1) * P], brng[:, 4 * par + k, :],
                                                 arng[:, 4 * par + k, :], start=True, stop=True)
                            last.then_inc(gmm_done, 1)
                    panel(2 * Q_PEER + 4 * tt + 3, c, (uT_r, sq_r), unit=4)
            with pe.Fori(0, 2 * EARLY - 4 * TT) as i:
                for j in range(4):
                    panel(i + (2 * Q_PEER + 4 * TT), j, (uT_r, sq_r), unit=4)
            pe.wait_ge(g_evac, 130)

            def up(q, ready=None):
                for j in range(8):
                    panel(q, j, (uT_r, sq_r), ready=None if j else ready)

            def down(s, q, par, g, r=None):
                pe.wait_ge(hid_ready[s], g * 8 + 8)
                for j in range(8):
                    panel(q, j, tuple(hid[par]))
                    if r:
                        behind(r, j)

            def hidden(s, q8, groups):
                up(q8, normed(4 if s == 1 else 6))
                with pe.Fori(0, groups // 2 - 1) as i:
                    up(i * 4 + (q8 + 1))
                    down(s, i * 4 + (q8 + 2), 0, i * 2)
                    up(i * 4 + (q8 + 3))
                    down(s, i * 4 + (q8 + 4), 1, i * 2 + 1)
                e = q8 + 2 * groups - 3
                up(e)
                down(s, e + 1, 0, groups - 2)
                down(s, e + 2, 1, groups - 1, 5 if s == 1 else 7)

            q = Q_PEER + EARLY
            down(0, q, 0, 0)
            with pe.Fori(0, EARLY // 2 - 1) as i:
                down(0, i * 2 + (q + 1), 1, i * 2 + 1)
                down(0, i * 2 + (q + 2), 0, i * 2 + 2)
            q += EARLY - 1
            with pe.Fori(0, (16 - EARLY) // 2) as i:
                up(i * 4 + q)
                down(0, i * 4 + (q + 1), 1, i * 2 + (EARLY - 1))
                up(i * 4 + (q + 2))
                down(0, i * 4 + (q + 3), 0, i * 2 + EARLY)
            down(0, Q_PEER + 31, 1, 15, 2)
            norm(2)

            def attention(s, r, q_qkv, q_wo):
                a = att[s]
                norm(r)
                for j in range(16):
                    panel(q_qkv + j // 8, j % 8, (uT_r, sq_r), ready=None if j else normed(r))
                def token_major(j):
                    pe.wait_ge(bank_free[j % BANKS], 2 * (q_qkv + 2) + j // BANKS + 1)
                    if 8 * s + j >= 2:
                        pe.wait_ge(vt_sb, 8 * s + j - 1)
                    for tt in range(TT):
                        last = t_.transpose(ps[:, 4 + j % 2, tt * P:(tt + 1) * P], vf[:, j % 2, tt * P:(tt + 1) * P], ident)
                    last.then_inc(vt_done, 1)

                for j in range(8):
                    panel(q_qkv + 2, j, (uT_r, sq_r))
                    if j:
                        token_major(j - 1)
                token_major(7)
                pe.wait_ge(vt_sb, 8 * s + 8)
                for b in range(BANKS):
                    pe.wait_ge(bank_free[b], 2 * (q_qkv + 3))

                def logits(n, par, hh):
                    pe.wait_ge(a["staged"], n * 3 + 3)
                    for qt in range(TT):
                        if not (isinstance(n, int) and n * 8 + 4 * hh + qt < 4):
                            pe.wait_ge(a["nm_ready"], n * 8 + (4 * hh + qt - 3))
                        t_.matmul(ps[:, qt, :], qs[64 * hh:64 * hh + 64, par, qt * P:(qt + 1) * P],
                                  ks[64 * hh:64 * hh + 64, par, :], start=True, stop=True).then_inc(a["lg_done"], 1)

                def values(n, par, hh, u, src):
                    for qt in range(TT):
                        pe.wait_ge(a["pn_ready"], u * 4 + (qt + 1))
                        pe.wait_ge(a["pt_ready"], u * 4 + (qt + 1))
                        for kt in range(TT):
                            last = t_.transpose(ps[:, 4 + qt % 2, kt * P:(kt + 1) * P],
                                                pb[:, par, src, qt, kt * P:(kt + 1) * P], ident)
                        last.then_inc(a["tr_done"], 1)
                    pe.wait_ge(a["pt_ready"], u * 4 + 6)
                    pe.wait_ge(a["o_ready"], u * 1 + 1)
                    bank = 6 + (hh if s == 0 else 0)
                    for kt in range(TT):
                        last = t_.matmul(ps[:, bank, :], vs[:, par, kt, :], pt[:, hh if s == 0 else par, kt, :],
                                         start=(kt == 0), stop=(kt == TT - 1))
                    last.then_inc(a["av_done"], 1)

                def bstat(u):
                    pe.wait_ge(rs_ms, u * 1 + RS_B)
                    pe.wait_ge(bsq_ready, u * 1 + 1)
                    t_.matmul(ps[:, 7, :], ones[:], sq[:, 0, :], start=True, stop=True).then_inc(stat_done, 1)

                if s == 0:
                    logits(0, 0, 0)
                    with pe.Fori(0, 3) as i:
                        logits(i * 2, 0, 1)
                        values(i * 2, 0, 0, i * 4, 0)
                        logits(i * 2 + 1, 1, 0)
                        values(i * 2, 0, 1, i * 4 + 1, 1)
                        logits(i * 2 + 1, 1, 1)
                        values(i * 2 + 1, 1, 0, i * 4 + 2, 0)
                        logits(i * 2 + 2, 0, 0)
                        values(i * 2 + 1, 1, 1, i * 4 + 3, 1)
                    logits(6, 0, 1)
                    values(6, 0, 0, 12, 0)
                    logits(7, 1, 0)
                    values(6, 0, 1, 13, 1)
                    logits(7, 1, 1)
                    values(7, 1, 0, 14, 0)
                    values(7, 1, 1, 15, 1)
                    pe.wait_ge(al_ready, 1)
                    for g in range(3):
                        for qt in range(TT):
                            last = t_.matmul(ps[:, g, qt * P:(qt + 1) * P], wg[:, g, qt:qt + 1].to_broadcast([P, P]), ident,
                                             start=True, stop=True)
                    last.then_inc(alb_done, 1)
                else:
                    logits(0, 0, 0)
                    logits(0, 0, 1)
                    with pe.Fori(0, 3) as i:
                        logits(i * 2 + 1, 1, 0)
                        logits(i * 2 + 1, 1, 1)
                        values(None, 0, 0, i * 2, 0)
                        bstat(i * 2)
                        logits(i * 2 + 2, 0, 0)
                        logits(i * 2 + 2, 0, 1)
                        values(None, 1, 0, i * 2 + 1, 0)
                        bstat(i * 2 + 1)
                    logits(7, 1, 0)
                    logits(7, 1, 1)
                    values(None, 0, 0, 6, 0)
                    bstat(6)
                    values(None, 1, 0, 7, 0)
                    bstat(7)
                pe.wait_ge(a["oT_ready"], 8)
                for j in range(8):
                    panel(q_wo, j, (uT_r, qT_r))
                    behind(4 if s == 0 else 6, j)

            attention(0, 3, Q_QKV_A, Q_WO_A)
            norm(4)
            hidden(1, Q_MLP_A, 4)
            attention(1, 5, Q_QKV_B, Q_WO_B)
            norm(6)
            hidden(2, Q_MLP_B, 4)
            norm(7)

        LAST = {1: Q_WOUT, 2: Q_PEER + 31, 4: Q_WO_A, 5: Q_MLP_A + 7, 6: Q_WO_B, 7: Q_MLP_B + 7}

        @block.scalar
        def _(act):
            for dst, src in ((cc[:], cols), (cst[:], consts), (ohs, oh), (rbs[:], rel), (lm, lmask),
                             (lam, blam)):
                act.dma_start(dst, src).then_inc(c_in, 16)
            act.dma_start(hT[:], xT).then_inc(x_in, 16)

            def taken(q8, j):
                act.wait_ge(gemm_done, q8 * 8 + (j + 1))

            def high(q8, j):
                if isinstance(q8, int) and 8 * q8 + j >= 8 * Q_END:
                    return
                act.wait_ge(w_slot[j % RING], q8 * 32 + 16 * (j // RING + 1))
                s_.activation(high_w[:, j % RING], ring[:, j % RING], ACT.Copy).then_inc(hi_ready, 1)

            def root(idx, n):
                s_.activation(small[:, 94:95], ones[:, 0:1], ACT.Sqrt).then_inc(warm, 1)
                act.wait_ge(warm, n + 1)
                act.wait_ge(rs_ms, idx + 1)
                s_.activation(sr[:], ms[:], ACT.Sqrt).then_inc(rs_sqrt, 1)

            def square(r, k):
                if k == 0:
                    if r:
                        act.wait_ge(stat_done, RS_NORM[r])
                    else:
                        act.wait_ge(x_in, 16)
                if r == 3:
                    act.wait_ge(u_ready, KT * 3 + k + 1)
                elif r:
                    act.wait_ge(bank_free[k % BANKS], 2 * LAST[r] + k // BANKS + 1)
                s_.activation(sq[:, k, :], hT[:, k, :], ACT.Square).then_inc(sq_ready, 1)

            def last_before(r, q):
                for j in range(KT):
                    taken(q, j)
                    high(q, j + 3)
                    if j:
                        square(r, j - 1)

            def norm(r):
                for k in range(0 if r in (0, 3) else KT - 1, KT):
                    square(r, k)
                root(RS_NORM[r], r + (r >= 1))
                if r in SPLIT_NORM and r:
                    high_x(r)

            def high_x(r):
                n = KT * SPLIT_NORM[r]
                if r < 2:
                    for k in range(KT):
                        act.wait_ge(upre, n + k + 1)
                        s_.activation(sq[:, k, :], sq[:, k, :], ACT.Identity,
                                      bias=ada[:, 24 * r + k:24 * r + k + 1]).then_inc(shifted, 1)
                for k in range(KT):
                    if r < 2:
                        act.wait_ge(shifted, n + k + 1)
                    else:
                        act.wait_ge(upre, n + k + 1)
                    s_.activation(uT_r[:, k, :], sq[:, k, :], ACT.Copy).then_inc(x_high, 1)

            act.wait_ge(ones_set, 1)
            act.wait_ge(c_in, 16 * 6)
            s_.activation(small[:, 0:8], cc[:, COLS["c"]:COLS["c"] + 8], ACT.Silu).then_inc(silu_c, 1)
            act.wait_ge(tab_done, 1)
            for n in range(4):
                s_.activation(gtab[:, n // 2, (n % 2) * 512:(n % 2) * 512 + 512], ps[0:16, 4 + n, :], ACT.Copy).then_inc(tab_sb, 1)
            act.wait_ge(tab_sb, 4)
            act.dma_start(btab.rearrange("s h x -> h s x"), gtab).then_inc(tab_dram, 16)
            act.wait_ge(lb_sem, 1)
            s_.activation(lbt[:, 0:16], lbt[:, 0:16], ACT.Exp).then_inc(lb_sem, 1)
            norm(0)
            for n in range(16):
                taken(n // 8, n % 8)
                s_.activation(ada[:, n:n + 1], ps[:, n % BANKS, 0:1], ACT.Identity, bias=col("ada_b", n)).then_inc(bank_free[n % BANKS], 1)
                if n >= 13:
                    high(Q_HEADS, n - 13)
            high_x(0)
            high(Q_HEADS, 3)
            for j in range(2):
                taken(Q_HEADS, j)
                high(Q_HEADS, 4 + j)

            def head_out(t):
                act.wait_ge(v_free, t * 1 + 3)
                act.wait_ge(og_ready, t * 1 + 2)
                s_.activation(ob[:], ps[:, 6, :], ACT.Copy).then_inc(o_copied, 1)
                act.wait_ge(o_copied, t * 1 + 2)
                s_.activation(osq[:], ob[:], ACT.Square).then_inc(osq_ready, 1)

            def head_root(t):
                act.wait_ge(rs_ms, t * 1 + (RS_HEAD + 1))
                s_.activation(sr[:], ms[:], ACT.Sqrt).then_inc(rs_sqrt, 1)

            def head(h, hh, q8, ahead, before=True):
                j0 = 4 * hh
                taken(q8, j0)
                act.wait_ge(f_ready, h * 1 + 1)
                act.wait_ge(og_ready, h * 1 + 1)
                s_.activation(eb[:], ps[:, 0, :], ACT.Exp, scale=-1.0).then_inc(bank_free[0], 1)
                taken(q8, j0 + 1)
                s_.activation(qb[:, hh, :], ps[:, 1, :], ACT.Copy).then_inc(bank_free[1], 1)
                taken(q8, j0 + 2)
                s_.activation(vb[:, hh], ps[:, 2, :].rearrange("p (a b) -> p a b", a=TT), ACT.Copy).then_inc(bank_free[2], 1)
                taken(q8, j0 + 3)
                s_.activation(gb[:, hh, :], ps[:, 3, :], ACT.Silu).then_inc(bank_free[3], 1)
                if ahead >= 1:
                    for j in (2, 3):
                        high(q8, j0 + 4 + j)
                act.wait_ge(f_ready, h * 1 + 2)
                s_.activation(lf[:], fb[:], ACT.Ln).then_inc(lf_ready, 1)
                act.wait_ge(b_ready, h * 1 + 1)
                s_.activation(eq[:, P:T], bb[:, P:T], ACT.Exp)
                for n in range(3):
                    s_.activation(ek[:, n * P:(n + 1) * P], bb[:, n * P:(n + 1) * P], ACT.Exp, scale=-1.0,
                                  bias=bb[:, n * P + P - 1:n * P + P])
                s_.activation(small[:, 40:42], bb[:, 2 * P - 1:3 * P:P], ACT.Exp).then_inc(ek_ready, 1)
                for n in range(7):
                    if n == 1 and before:
                        head_out(h + (-1))
                    if n == 2:
                        act.wait_ge(off_done, h * 2 + 1)
                        s_.activation(soff[:, hh, 0:2, :], ps[:, 5, 0:2 * P].rearrange("p (a b) -> p a b", a=2), ACT.Copy).then_inc(soff_ready, 1)
                    if n == 3:
                        act.wait_ge(off_done, h * 2 + 2)
                        s_.activation(soff[:, hh, 2:6, :], ps[:, 6, :].rearrange("p (a b) -> p a b", a=4), ACT.Copy).then_inc(soff_ready, 1)
                    if n == 4 and before:
                        head_root(h + (-1))
                    act.wait_ge(d_ready, h * 7 + (n + 1))
                    s_.activation(db[:, n % 2, :], db[:, n % 2, :], ACT.Exp).then_inc(e_ready, 1)
                if ahead >= 2:
                    for j in (0, 1):
                        taken(q8, j0 + 4 + j)
                        high(q8, j0 + 8 + j)

            head(0, 0, Q_HEADS, 3, before=False)
            with act.Fori(0, HEADS // 2 - 2) as i:
                head(i * 2 + 1, 1, i + Q_HEADS, 2)
                head(i * 2 + 2, 0, i + (Q_HEADS + 1), 2)
            head(5, 1, Q_HEADS + 2, 2)
            head(6, 0, Q_HEADS + 3, 1)
            head(7, 1, Q_HEADS + 3, 0)
            head_out(7)
            head_root(7)

            with act.Fori(0, KT) as i:
                q8 = i + Q_GATES
                taken(q8, 0)
                act.wait_ge(bank_free[1], q8 * 2)
                s_.activation(sg[:, 0, :], ps[:, 0, :], ACT.Sigmoid).then_inc(bank_free[0], 1)
                n = 0
                for j in range(2, 8):
                    taken(q8, j)
                    if j in (3, 5):
                        dst = sga if j == 3 else sgb
                        s_.activation(dst[:, bass.ds(i, 1), :], ps[:, j % BANKS, :], ACT.Sigmoid).then_inc(bank_free[j % BANKS], 1)
                    else:
                        s_.activation(ada[:, bass.ds(i * 4 + (16 + n), 1)], ps[:, j % BANKS, 0:1], ACT.Identity,
                                      bias=cc[:, bass.ds(i * 4 + (COLS["ada_b"] + 16 + n), 1)]).then_inc(bank_free[j % BANKS], 1)
                        n += 1
            for j in range(3):
                high(Q_WA, j)
            act.wait_ge(stat_done, RS_LN)
            for k in range(KT):
                act.wait_ge(xc_ready, k + 1)
                s_.activation(sq[:, k, :], cv[:, k, :], ACT.Square).then_inc(lnsq_ready, 1)
                if k in (3, 5, 7):
                    taken(Q_WA, (k - 3) // 2)
                    high(Q_WA, (k - 3) // 2 + 3)
            for j in range(3, 6):
                if j == 4:
                    root(RS_LN, 1)
                taken(Q_WA, j)
                high(Q_WA, j + 3)
            for j in range(6, 8):
                taken(Q_WA, j)
                high(Q_WA, j + 3)
            for k in range(KT):
                act.wait_ge(cvn_ready, k + 1)
                s_.activation(cv[:, k, :], cv[:, k, :], ACT.Silu, bias=col("ln_b", k)).then_inc(cvs_ready, 1)
            for j in range(KT):
                taken(Q_WB, j)
                high(Q_WB, j + 3)
            last_before(1, Q_WOUT)
            norm(1)

            for j in range(16):
                taken(Q_WQ, j)
                s_.activation(qpeer[:, j, :], ps[:, j % BANKS, :], ACT.Copy).then_inc(bank_free[j % BANKS], 1)
                high(Q_WQ, j + 3)
            act.dma_start(ky, keysT).then_inc(ky_in, 16)
            act.wait_ge(tab_dram, 16)
            act.dma_start(strips_dram, bass.AP(tensor=btab.tensor, offset=P - 1, ap=[[1024, 2 * A_HEADS], [-1, P], [1, STRIP]]))\
               .then_inc(strips_out, 16)
            for hp in range(16):
                act.wait_ge(sc_done, hp + 1)
                s_.activation(qpeer[:, hp, :], ps[:, hp % 4, :], ACT.Copy).then_inc(sc_sb, 1)

            def early(b4, j):
                act.wait_ge(gemm_done, b4 * 4 + (8 * Q_PEER + j + 1))
                act.wait_ge(a_out, b4 * 64 + (16 * j + 16))
                s_.activation(act_out[:, 0, :], ps[:, j, :], ACT.Gelu).then_inc(bank_free[j], 1)
                k = (j + 3) % RING
                act.wait_ge(w_slot[k], b4 * 16 + (16 * (2 * Q_PEER + (j + 3) // RING) + 16))
                s_.activation(high_w[:, k], ring[:, k], ACT.Copy).then_inc(hi_ready, 1)
                act.wait_ge(bank_free[j], b4 * 1 + (2 * Q_PEER + 1))
                act.dma_start(adram[bass.ds(b4 * 4 + j, 1)].rearrange("n p t -> p n t"), act_out[:])\
                   .then_inc(a_out, 16)

            with act.Fori(0, TT) as tt:
                with act.Fori(0, 2) as i:
                    for j in range(4):
                        early(tt * 4 + i, j)
                early(tt * 4 + 2, 0)
                early(tt * 4 + 2, 1)
                act.wait_ge(gate_in, tt * 1 + 1)
                s_.activation(slot[:, 2, :], slot[:, 2, :], ACT.Exp).then_inc(gate_exp, 1)
                early(tt * 4 + 2, 2)
                early(tt * 4 + 2, 3)
                act.wait_ge(g_out, tt * 64 + 16)
                for c in range(4):
                    with act.Fori(0, 4) as i:
                        for par in range(2):
                            act.wait_ge(gmm_done, tt * 32 + i * 2 + (8 * c + par + 3))
                            s_.activation(gbuf[:, :, bass.ds(i * 8 + (32 * c + 4 * par), 4)].rearrange("p i t -> p t i"),
                                          ps[:, 6 + par, :].rearrange("p (a b) -> p a b", a=4), ACT.Copy).then_inc(g_evac, 1)
                    early(tt * 4 + 3, c)
                act.wait_ge(g_evac, tt * 32 + 34)
                for c in range(4):
                    act.dma_start(gdram[bass.ds(tt, 1), 32 * c:32 * c + 32].rearrange("s i j t -> j (s i) t"),
                                  gbuf[:, 32 * c:32 * c + 32, :]).then_inc(g_out, 16)
            with act.Fori(0, EARLY - 2 * TT) as i:
                for j in range(4):
                    early(i + 4 * TT, j)

            def gates(g, par):
                for k in range(8):
                    act.dma_start(gi[:, par, k, :].rearrange("p (a t) -> p a t", a=TT),
                                  gdram[:, bass.ds(g * 8 + k, 1)].rearrange("a i j t -> j (i a) t")).then_inc(g_in[par], 16)

            def fetch(m8, j, first=False):
                if not first:
                    act.wait_ge(hid_ready[0], m8 * 8 + (j - 3))
                act.dma_start(gel[:, j % 4:j % 4 + 1, :], adram[bass.ds(m8 * 8 + j, 1)].rearrange("n p t -> p n t")
                              if not isinstance(m8, int) else adram[8 * m8 + j:8 * m8 + j + 1].rearrange("n p t -> p n t"))\
                   .then_inc(a_in[j % 4], 16)

            def up(s, q, g, par, first=False, fetch=True):
                if fetch and s == 0:
                    act.wait_ge(hid_ready[s], g * 8)
                    gates(g + 1, 1 - par)
                for j in range(8):
                    taken(q, j)
                    if not (first and j < 4):
                        act.wait_ge(hid_ready[s], g * 8 + (j - 3))
                    s_.activation(gel[:, j % 4, :], ps[:, j % BANKS, :], ACT.Gelu if s == 0 else ACT.Relu).then_inc(bank_free[j % BANKS], 1)
                    high(q, j + 3)

            def down(q):
                for j in range(8):
                    taken(q, j)
                    high(q, j + 3)

            def hidden(s, q8, groups):
                up(s, q8, 0, 0, first=True)
                with act.Fori(0, groups // 2 - 1) as i:
                    up(s, i * 4 + (q8 + 1), i * 2 + 1, 1)
                    down(i * 4 + (q8 + 2))
                    up(s, i * 4 + (q8 + 3), i * 2 + 2, 0)
                    down(i * 4 + (q8 + 4))
                e = q8 + 2 * groups - 3
                up(s, e, groups - 1, 1, fetch=False)
                down(e + 1)
                last_before(5 if s == 1 else 7, e + 2)

            def early_down(q, g, par, more=True):
                act.wait_ge(hid_ready[0], g * 8 + 8)
                gates(g + 2, par)
                for j in range(8):
                    if more or j < 4:
                        fetch(g + (1 + (j + 4) // 8), (j + 4) % 8)
                    taken(q, j)
                    high(q, j + 3)

            act.wait_ge(g_out, 272)
            gates(0, 0)
            gates(1, 1)
            act.wait_ge(a_out, 16 * 8 + 16)
            for j in range(8):
                fetch(0, j, first=j < 4)
            with act.Fori(0, EARLY - 2 * TT) as i:
                for j in range(4):
                    early(i + (EARLY + 2 * TT), j)
            act.wait_ge(a_out, 16 * (8 * EARLY) + 16)
            for j in range(4):
                fetch(1, j)
            q = Q_PEER + EARLY
            early_down(q, 0, 0)
            with act.Fori(0, EARLY // 2 - 2) as i:
                early_down(i * 2 + (q + 1), i * 2 + 1, 1)
                early_down(i * 2 + (q + 2), i * 2 + 2, 0)
            early_down(q + EARLY - 3, EARLY - 3, 1)
            early_down(q + EARLY - 2, EARLY - 2, 0, more=False)
            q += EARLY - 1
            with act.Fori(0, (16 - EARLY) // 2 - 1) as i:
                up(0, i * 4 + q, i * 2 + EARLY, 0)
                down(i * 4 + (q + 1))
                up(0, i * 4 + (q + 2), i * 2 + (EARLY + 1), 1)
                down(i * 4 + (q + 3))
            up(0, Q_PEER + 27, 14, 0)
            down(Q_PEER + 28)
            up(0, Q_PEER + 29, 15, 1, fetch=False)
            down(Q_PEER + 30)
            last_before(2, Q_PEER + 31)
            norm(2)

            def attention(s, r, q_qkv):
                a = att[s]
                norm(r)

                def token_major(j):
                    act.wait_ge(vt_done, 8 * s + j + 1)
                    s_.activation(vtok[:, :, j * P:(j + 1) * P], ps[:, 4 + j % 2, :].rearrange("p (a b) -> p a b", a=TT),
                                  ACT.Copy).then_inc(vt_sb, 1)

                for j in range(24):
                    taken(q_qkv, j)
                    if j < 8:
                        ins = s_.activation(qT[:, j, :], ps[:, j % BANKS, :], ACT.Copy, scale=0.125)
                    elif j < 16:
                        ins = s_.activation(kT[:, j - 8, :], ps[:, j % BANKS, :], ACT.Copy)
                    else:
                        if j >= 18:
                            act.wait_ge(vt_done, 8 * s + j - 17)
                        ins = s_.activation(vf[:, j % 2, :], ps[:, j % BANKS, :], ACT.Copy)
                    ins.then_inc(bank_free[j % BANKS], 1)
                    high(q_qkv, j + 3)
                    if j > 16:
                        token_major(j - 17)
                token_major(7)
                if s == 0:
                    act.wait_ge(strips_out, 16)

                def strips(u, hh):
                    act.dma_start(strip[:, hh:hh + 1, :], strips_dram[bass.ds(u + s * A_HEADS, 1)].rearrange("u p y -> p u y"))\
                       .then_inc(strip_in[s][hh], 16)

                def exps(n, par, hh, more=True):
                    for qt in range(TT):
                        act.wait_ge(a["nm_ready"], n * 8 + (4 * hh + qt + 1))
                        s_.activation(pb[:, par, hh, qt, :], pb[:, par, hh, qt, :], ACT.Exp, bias=nm[:, hh, qt:qt + 1],
                                      accum_out=zt[:, hh, qt:qt + 1]).then_inc(a["p_ready"], 1)
                    if more:
                        strips(n * 2 + (hh + 2), hh)

                def values(n, par, hh, u):
                    for qt in range(TT):
                        act.wait_ge(a["tr_done"], u * 4 + (qt + 1))
                        s_.activation(pt[:, hh if s == 0 else par, :, qt * P:(qt + 1) * P],
                                      ps[:, 4 + qt % 2, :].rearrange("p (a b) -> p a b", a=TT), ACT.Copy).then_inc(a["pt_ready"], 1)
                    act.wait_ge(a["av_done"], u * 1 + 1)
                    if s == 0:
                        rows = slice(64 * hh, 64 * hh + 64)
                        s_.activation(qT[rows, bass.ds(n, 1), :] if not isinstance(n, int) else qT[rows, n:n + 1, :],
                                      ps[rows, 6 + hh, :], ACT.Copy).then_inc(a["o_ready"], 1)
                    else:
                        s_.activation(sq[:, 1 + par, :], ps[:, 6, :], ACT.Copy).then_inc(a["o_ready"], 1)
                        act.wait_ge(a["o_ready"], u * 1 + 2)
                        act.wait_ge(stat_done, u * 1 + RS_B)
                        s_.activation(sq[:, 0, :], sq[:, 1 + par, :], ACT.Square).then_inc(bsq_ready, 1)
                        act.wait_ge(rs_ms, u * 1 + (RS_B + 1))
                        s_.activation(sr[:], ms[:], ACT.Sqrt).then_inc(rs_sqrt, 1)

                def stage(n, par):
                    sl = slice(n, n + 1) if isinstance(n, int) else bass.ds(n, 1)
                    s_.activation(qs[:, par:par + 1, :], qT[:, sl, :], ACT.Copy).then_inc(a["staged"], 1)
                    s_.activation(ks[:, par:par + 1, :], kT[:, sl, :], ACT.Copy).then_inc(a["staged"], 1)
                    vsl = slice(n * P, n * P + P) if isinstance(n, int) else bass.ds(n * P, P)
                    s_.activation(vs[:, par], vtok[:, :, vsl], ACT.Copy).then_inc(a["staged"], 1)

                strips(0, 0)
                strips(1, 1)
                for b in range(BANKS):
                    act.wait_ge(bank_free[b], 2 * (q_qkv + 3))
                act.wait_ge(vt_sb, 8 * s + 8)
                stage(0, 0)
                stage(1, 1)
                if s == 0:
                    exps(0, 0, 0)
                    with act.Fori(0, 3) as i:
                        exps(i * 2, 0, 1)
                        values(i * 2, 0, 0, i * 4)
                        exps(i * 2 + 1, 1, 0)
                        values(i * 2, 0, 1, i * 4 + 1)
                        stage(i * 2 + 2, 0)
                        exps(i * 2 + 1, 1, 1)
                        values(i * 2 + 1, 1, 0, i * 4 + 2)
                        exps(i * 2 + 2, 0, 0)
                        values(i * 2 + 1, 1, 1, i * 4 + 3)
                        stage(i * 2 + 3, 1)
                    exps(6, 0, 1)
                    values(6, 0, 0, 12)
                    exps(7, 1, 0, more=False)
                    values(6, 0, 1, 13)
                    exps(7, 1, 1, more=False)
                    values(7, 1, 0, 14)
                    values(7, 1, 1, 15)
                    act.wait_ge(a["lse"], 1)
                    s_.activation(zs[:, 2], zs[:, 1], ACT.Ln).then_inc(a["lse"], 1)
                    act.wait_ge(a["lse"], 3)
                    s_.activation(zs[:, 1], zs[:, 0], ACT.Exp).then_inc(a["lse"], 1)
                    act.wait_ge(alb_done, 1)
                    for g in range(3):
                        s_.activation(alb[:, g, :], ps[:, g, :], ACT.Copy).then_inc(alb_sb, 1)
                else:
                    exps(0, 0, 0)
                    exps(0, 0, 1)
                    with act.Fori(0, 3) as i:
                        exps(i * 2 + 1, 1, 0)
                        exps(i * 2 + 1, 1, 1)
                        values(None, 0, 0, i * 2)
                        stage(i * 2 + 2, 0)
                        exps(i * 2 + 2, 0, 0)
                        exps(i * 2 + 2, 0, 1)
                        values(None, 1, 0, i * 2 + 1)
                        stage(i * 2 + 3, 1)
                    exps(7, 1, 0, more=False)
                    exps(7, 1, 1, more=False)
                    values(None, 0, 0, 6)
                    values(None, 1, 0, 7)

            attention(0, 3, Q_QKV_A)
            last_before(4, Q_WO_A)
            norm(4)
            hidden(1, Q_MLP_A, 4)
            act.wait_ge(lb_sem, 3)
            s_.activation(lamc[:, 0:2], lamc[:, 0:2], ACT.Exp).then_inc(lb_sem, 1)
            attention(1, 5, Q_QKV_B)
            last_before(6, Q_WO_B)
            norm(6)
            hidden(2, Q_MLP_B, 4)
            norm(7)

        @block.vector
        def _(ve):
            S = Steps(ve, dve_step)

            def taken(q8, j):
                ve.wait_ge(gemm_done, q8 * 8 + (j + 1))

            def evacuated(q8, j):
                ve.wait_ge(bank_free[j % BANKS], q8 * 2 + (j // BANKS + 1))

            def carry_waits():
                ve.sem_inc(carried, 1)

            def newton(idx):
                ve.wait_ge(rs_sqrt, idx * 1 + 1)
                S.done(v_.reciprocal(rt[:], sr[:]))
                S.done(v_.tensor_tensor(rstd[:], rt[:], rt[:], ALU.mult))
                S.done(v_.tensor_tensor(rstd[:], rstd[:], ms[:], ALU.mult))
                S.done(v_.tensor_scalar(rstd[:], rstd[:], -0.5, 1.5, ALU.mult, ALU.add))
                S.done(v_.tensor_tensor(rstd[:], rstd[:], rt[:], ALU.mult))

            def rsqrt(idx, width, bank=4):
                ve.wait_ge(stat_done, idx * 1 + 1)
                v_.tensor_scalar(ms[:], ps[:, bank, :], 1.0 / width, EPS, ALU.mult, ALU.add).then_inc(rs_ms, 1)
                newton(idx)

            def split_to(high, low, src):
                S.done(v_.tensor_scalar(high, src, 1.0, None, ALU.mult))
                return v_.tensor_tensor(low, src, high, ALU.subtract)

            def norm(r, gain):
                if r:
                    rsqrt(RS_NORM[r], D)
                for k in range(KT):
                    v_.scalar_tensor_tensor(out=(hT if r == 2 else sq)[:, k, :], in0=hT[:, k, :], scalar=gain(k),
                                            in1=rstd[:], op0=ALU.mult, op1=ALU.mult).then_inc(upre if r in SPLIT_NORM else u_ready, 1)
                if r in SPLIT_NORM:
                    for k in range(KT):
                        ve.wait_ge(x_high, KT * SPLIT_NORM[r] + k + 1)
                        v_.tensor_tensor((sq_r if r else ulo)[:, k, :], sq[:, k, :], uT_r[:, k, :], ALU.subtract).then_inc(u_ready, 1)

            v_.memset(ones[:], 1.0).then_inc(ones_set, 1)
            ve.wait_ge(ones_set, 1)
            S.done(v_.memset(sd[:], 0.0))
            ve.wait_ge(c_in, 16 * 6)
            l0 = cc[:, COLS["lb0"]:COLS["lb0"] + 8]
            l1 = cc[:, COLS["lb1"]:COLS["lb1"] + 8]
            S.done(v_.tensor_tensor(lbt[:, 16:24], l0, l1, ALU.max))
            S.done(v_.tensor_tensor(lbt[:, 0:8], l0, lbt[:, 16:24], ALU.subtract))
            v_.tensor_tensor(lbt[:, 8:16], l1, lbt[:, 16:24], ALU.subtract).then_inc(lb_sem, 1)
            ve.wait_ge(lb_sem, 2)
            S.done(v_.tensor_tensor(lbt[:, 16:24], lbt[:, 0:8], lbt[:, 8:16], ALU.add))
            S.done(v_.reciprocal(lbt[:, 16:24], lbt[:, 16:24]))
            S.done(v_.tensor_tensor(small[:, 8:16], lbt[:, 0:8], lbt[:, 16:24], ALU.mult))
            S.done(v_.tensor_scalar(small[:, 16:24], small[:, 8:16], -1.0, 1.0, ALU.mult, ALU.add))
            for n in range(2):
                S.done(v_.tensor_tensor_reduce(out=lamt[:], in0=lam[:, 2 * n, :], in1=lam[:, 2 * n + 1, :], scale=1.0, scalar=0.0,
                                               op0=ALU.mult, op1=ALU.add, accum_out=lamc[:, n:n + 1]))
            v_.tensor_scalar(subc[:], col("subln"), 1.0 - LAMBDA_INIT, None, ALU.mult).then_inc(lb_sem, 1)

            def gain_of(r):
                name = "norm1" if r == 0 else "norm2"
                S.done(v_.tensor_scalar(small[:, 48:56], ada[:, 24 * r + 8:24 * r + 16], 1.0, None, ALU.add))
                S.done(v_.tensor_tensor(small[:, 24 + 8 * r:32 + 8 * r], small[:, 48:56], cc[:, COLS[name]:COLS[name] + 8], ALU.mult))

            rsqrt(0, D)
            for j in range(4):
                evacuated(1, 4 + j)
            gain_of(0)
            ve.wait_ge(tab_dram, 16)
            norm(0, lambda k: small[:, 24 + k:25 + k])

            def seg(x, L):
                y = x.rearrange("p (s w) -> p s w", w=2 * L)
                n = T // (2 * L)
                return y[:, :, 0:L], y[:, :, L:2 * L], y[:, :, L - 1:L].broadcast_to([P, n, L])

            def head_mean(t):
                ve.wait_ge(stat_done, t * 1 + (RS_HEAD + 1))
                v_.tensor_scalar(ms[:], ps[:, 4, :], 1.0 / P, EPS, ALU.mult, ALU.add).then_inc(rs_ms, 1)

            def head_gate(t, hh):
                newton(t + RS_HEAD)
                ve.wait_ge(o_copied, t * 1 + 2)
                S.done(v_.scalar_tensor_tensor(out=osc, in0=ob[:], scalar=cc[:, t + COLS["hgn"]:t + COLS["hgn"] + 1] if isinstance(t, int)
                                               else cc[:, bass.ds(t * 1 + COLS["hgn"], 1)], in1=rstd[:],
                                               op0=ALU.mult, op1=ALU.mult))
                to = og[:, t:t + 1, :] if isinstance(t, int) else og[:, bass.ds(t, 1), :]
                v_.tensor_tensor(to, osc.unsqueeze(1), gb[:, hh, :].unsqueeze(1), ALU.mult).then_inc(og_ready, 1)

            def head(h, hh, q8, before=True):
                j0 = 4 * hh
                evacuated(q8, j0)
                S.done(v_.tensor_scalar(eb[:], eb[:], 1.0, None, ALU.add))
                S.done(v_.reciprocal(fb[:], eb[:]))
                v_.tensor_scalar(fb[:], fb[:], small[:, bass.ds(h * 1 + 16, 1)], small[:, bass.ds(h * 1 + 8, 1)],
                                 ALU.mult, ALU.add).then_inc(f_ready, 1)
                ve.wait_ge(f_ready, h * 1 + 2)
                S.done(v_.tensor_scalar(kb[:, hh, :], fb[:], -1.0, 1.0, ALU.mult, ALU.add))
                ve.wait_ge(lf_ready, h * 1 + 1)
                for n in range(TT):
                    ins = v_.tensor_tensor_scan(out=bb[:, n * P:(n + 1) * P], data0=ones[:], data1=lf[:, n * P:(n + 1) * P],
                                                initial=0.0, op0=ALU.mult, op1=ALU.add)
                ins.then_inc(b_ready, 1)
                ve.wait_ge(b_ready, h * 1 + 1)

                def differences(n):
                    l, r, m = seg(bb, LEVELS[n])
                    dl, dr, _ = seg(db[:, n % 2, :], LEVELS[n])
                    v_.tensor_tensor(dl, m, l, ALU.subtract)
                    v_.tensor_tensor(dr, r, m, ALU.subtract).then_inc(d_ready, 1)

                differences(0)
                ve.wait_ge(ek_ready, h * 1 + 1)
                evacuated(q8, j0 + 1)
                q, k = qb[:, hh, :], kb[:, hh, :]
                S.mark(v_.tensor_tensor(qoff[:, 0:2, :], q[:, P:3 * P].rearrange("p (a b) -> p a b", a=2), eq[:, P:3 * P].rearrange("p (a b) -> p a b", a=2), ALU.mult))
                S.mark(v_.tensor_tensor(qoff[:, 3, :], q[:, 3 * P:], eq[:, 3 * P:], ALU.mult))
                S.done(v_.tensor_tensor(koff[:, 0:3, :], k[:, 0:3 * P].rearrange("p (a b) -> p a b", a=3), ek[:, 0:3 * P].rearrange("p (a b) -> p a b", a=3), ALU.mult))
                v_.tensor_scalar(qoff[:, 2, :], qoff[:, 3, :], small[:, 41:42], None, ALU.mult)
                v_.tensor_scalar(koff[:, 3, :], koff[:, 0, :], small[:, 40:41], None, ALU.mult).then_inc(off_ready, 1)
                for n in range(7):
                    if n == 2 and before:
                        head_mean(h + (-1))
                    if n == 5 and before:
                        head_gate(h + (-1), 1 - hh)
                    if n < 6:
                        if n:
                            ve.wait_ge(x_ready, h * 7 + n)
                        differences(n + 1)
                    ve.wait_ge(e_ready, h * 7 + (n + 1))
                    dl, dr, _ = seg(db[:, n % 2, :], LEVELS[n])
                    ql, qr, _ = seg(q, LEVELS[n])
                    kl, kr, _ = seg(k, LEVELS[n])
                    xl, xr, _ = seg(sq[:, n, :], LEVELS[n])
                    v_.tensor_tensor(xl, dl, kl, ALU.mult)
                    v_.tensor_tensor(xr, dr, qr, ALU.mult).then_inc(x_ready, 1)
                ve.wait_ge(v_free, h * 1 + 1)
                for n in range(8):
                    ve.wait_ge(lvl_done, h * 8 + (n + 1))
                    if n:
                        ve.wait_ge(lvl_evac, h * 8 + (n + 1))
                    bank = 7 if n % 2 == 0 else 5
                    carry_waits()
                    v_.copy_predicated(sd[:, hh], lm[:, n, :].unsqueeze(1).broadcast_to([P, TT, P]),
                                       ps[:, bank, :].rearrange("p (a b) -> p a b", a=TT)).then_inc(lvl_evac, 1)

            head(0, 0, Q_HEADS, before=False)
            with S.loop(HEADS // 2 - 2, 24) as i:
                head(i * 2 + 1, 1, i + Q_HEADS)
                head(i * 2 + 2, 0, i + (Q_HEADS + 1))
            head(5, 1, Q_HEADS + 2)
            head(6, 0, Q_HEADS + 3)
            taken(Q_HEADS + 3, 7)
            for k in range(KT):
                v_.tensor_tensor(uT[:, k, :], uT_r[:, k, :], ulo[:, k, :], ALU.add).then_inc(u_ready, 1)
            head(7, 1, Q_HEADS + 3)
            head_mean(7)
            head_gate(7, 1)

            PAD = CONV_K - 1
            S.done(v_.memset(glu[:, 0:PAD], 0.0))
            with S.loop(KT, CONV_K - 1) as i:
                q8 = i + Q_GATES
                taken(q8, 1)
                evacuated(q8, 0)
                v_.tensor_tensor(glu[:, PAD:PAD + T], ps[:, 1, :], sg[:, 0, :], ALU.mult).then_inc(bank_free[1], 1)
                ve.wait_ge(bank_free[1], q8 * 2 + 1)
                c = cv[:, bass.ds(i, 1), :]

                def tap(n):
                    return cc[:, bass.ds(i * CONV_K + (COLS["conv_w"] + n), 1)]

                S.done(v_.tensor_scalar(c, glu[:, 0:T].unsqueeze(1), tap(0), cc[:, bass.ds(i * 1 + COLS["conv_b"], 1)], ALU.mult, ALU.add))
                for n in range(1, CONV_K):
                    ins = v_.scalar_tensor_tensor(out=c, in0=glu[:, n:n + T].unsqueeze(1), scalar=tap(n), in1=c, op0=ALU.mult, op1=ALU.add)
                    if n < CONV_K - 1:
                        S.done(ins)
                    else:
                        ins.then_inc(cv_ready, 1)
                        ve.wait_ge(cv_ready, i * 1 + 1)
            taken(Q_GATES + 7, 7)
            for k in range(KT):
                split_to(uT_r[:, k, :], og_r[:, k, :], og[:, k, :]).then_inc(in_ready, 1)
            ve.wait_ge(mean_done, 1)
            S.done(v_.tensor_scalar(mu[:], ps[:, 5, :], 1.0 / D, None, ALU.mult))
            for k in range(KT):
                v_.tensor_tensor(cv[:, k, :], cv[:, k, :], mu[:], ALU.subtract).then_inc(xc_ready, 1)
            for j in range(4):
                taken(Q_WA, j)
                v_.tensor_tensor(sga[:, j, :], sga[:, j, :], ps[:, j % BANKS, :], ALU.mult).then_inc(bank_free[j % BANKS], 1)
            rsqrt(RS_LN, D)
            for k in range(KT):
                v_.scalar_tensor_tensor(out=cv[:, k, :], in0=cv[:, k, :], scalar=col("ln_g", k), in1=rstd[:],
                                        op0=ALU.mult, op1=ALU.mult).then_inc(cvn_ready, 1)
                if k % 2:
                    j = 4 + k // 2
                    taken(Q_WA, j)
                    v_.tensor_tensor(sga[:, j, :], sga[:, j, :], ps[:, j % BANKS, :], ALU.mult).then_inc(bank_free[j % BANKS], 1)
            for k in range(KT):
                ve.wait_ge(cvs_ready, k + 1)
                split_to(cvh[:, k, :], cv_r[:, k, :], cv[:, k, :]).then_inc(in_ready, 1)
            for j in range(KT):
                taken(Q_WB, j)
                v_.tensor_tensor(sgb[:, j, :], sgb[:, j, :], ps[:, j % BANKS, :], ALU.mult).then_inc(bank_free[j % BANKS], 1)
                ve.wait_ge(bank_free[j % BANKS], 2 * Q_WB + j // BANKS + 1)
                S.done(v_.tensor_tensor(sga[:, j, :], sga[:, j, :], sgb[:, j, :], ALU.add))
                split_to(uT_r[:, j, :], sga_r[:, j, :], sga[:, j, :]).then_inc(m_ready, 1)

            def residual(q8, j, gain=None):
                taken(q8, j)
                if gain is not None:
                    ins = v_.scalar_tensor_tensor(out=hT[:, j, :], in0=ps[:, j % BANKS, :], scalar=ada[:, gain + j:gain + j + 1],
                                                  in1=hT[:, j, :], op0=ALU.mult, op1=ALU.add)
                else:
                    ins = v_.tensor_tensor(hT[:, j, :], ps[:, j % BANKS, :], hT[:, j, :], ALU.add)
                ins.then_inc(bank_free[j % BANKS], 1)

            for j in range(KT):
                residual(Q_WOUT, j, 16)
            gain_of(1)
            norm(1, lambda k: small[:, 32 + k:33 + k])

            def best(values_of, spare, vals, idx, first=False):
                S.done(v_.max(vals[:, 0:8], values_of))
                v_.max_index(idx[:, 0:8], vals[:, 0:8], values_of)
                S.done(v_.match_replace(spare, vals[:, 0:8], values_of, LOWEST))
                S.done(v_.max(vals[:, 8:16], spare))
                return v_.max_index(idx[:, 8:16], vals[:, 8:16], spare)

            for tt in range(TT):
                for hp in range(16):
                    if tt == 0:
                        ve.wait_ge(sc_sb, hp + 1)
                    ins = best(qpeer[:, hp, tt * P:(tt + 1) * P], srep[:], sc16[:, hp, :], ix16u[:, hp, :])
                S.done(ins)
                S.done(v_.tensor_copy(ix16[:], ix16u[:]))
                hsc = sc16.rearrange("p (h s) k -> p h s k", s=2)
                S.done(v_.tensor_tensor(cand.rearrange("p (h i j) -> p h i j", h=PEER_HEADS, i=TOPK),
                                        hsc[:, :, 0, :].unsqueeze(3).broadcast_to([P, PEER_HEADS, TOPK, TOPK]),
                                        hsc[:, :, 1, :].unsqueeze(2).broadcast_to([P, PEER_HEADS, TOPK, TOPK]), ALU.add))
                if tt:
                    ve.wait_ge(hot_ready, tt * 32)
                for h in range(PEER_HEADS):
                    S.mark(best(cand[:, 256 * h:256 * h + 256], crep[:], tops[:, h, :], posu[:, h * TOPK:(h + 1) * TOPK]))
                S.wait()
                S.mark(v_.tensor_scalar(piu[:, 0, :], posu[:], 4, None, ALU.logical_shift_right))
                S.done(v_.tensor_scalar(piu[:, 1, :], posu[:], 15, None, ALU.bitwise_and))
                S.done(v_.tensor_copy(pif, piu[:]))
                hix = ix16.rearrange("p (h s) k -> p h s k", s=2)
                for s in range(2):
                    o3 = oneh.rearrange("p (n x) -> p n x", x=TOPK)
                    S.done(v_.tensor_tensor(o3, pif[:, s, :].unsqueeze(2).broadcast_to([P, SLOTS, TOPK]),
                                            iota[:, 0:TOPK].unsqueeze(1).broadcast_to([P, SLOTS, TOPK]), ALU.is_equal))
                    o4 = oneh.rearrange("p (h n x) -> p h n x", h=PEER_HEADS, x=TOPK)
                    S.done(v_.tensor_tensor(o4, o4, hix[:, :, s, :].unsqueeze(2).broadcast_to([P, PEER_HEADS, TOPK, TOPK]), ALU.mult))
                    v_.tensor_reduce(slot[:, s, :], o3, AX.X, ALU.add).then_inc(slot_ready, 1)
                    ve.wait_ge(slot_ready, tt * 3 + (s + 1))
                g3 = slot[:, 2, :].rearrange("p (h k) -> p h k", k=TOPK)
                v_.tensor_tensor(g3, tops[:], tops[:, :, 0:1].broadcast_to([P, PEER_HEADS, TOPK]), ALU.subtract).then_inc(gate_in, 1)
                ve.wait_ge(gate_exp, tt * 1 + 1)
                S.done(v_.tensor_reduce(gsum[:, :, 0], g3, AX.X, ALU.add))
                S.done(v_.reciprocal(gsum[:, :, 1], gsum[:, :, 0]))
                v_.tensor_tensor(g3, g3, gsum[:, :, 1:2].broadcast_to([P, PEER_HEADS, TOPK]), ALU.mult).then_inc(slot_ready, 1)
                ve.wait_ge(slot_tr, tt * 1 + 1)
                v_.tensor_copy(slotT[:], ps[:, 4, 0:3 * P].rearrange("p (a b) -> p a b", a=3)).then_inc(slot_sb, 1)
                ve.wait_ge(slot_sb, tt * 1 + 1)
                with ve.Fori(0, 16) as i:
                    for par in range(2):
                        ve.wait_ge(gmm_done, i * 2 + (tt * 32 + par + 1))
                        for k in range(4):
                            t = i * 8 + (4 * par + k)
                            ins = v_.tensor_scalar(arng[:, 4 * par + k, :], iota[:], slotT[:, 0, bass.ds(t, 1)],
                                                   slotT[:, 2, bass.ds(t, 1)], ALU.is_equal, ALU.mult)
                            ins = v_.tensor_scalar(brng[:, 4 * par + k, :], iota[:], slotT[:, 1, bass.ds(t, 1)], None, ALU.is_equal)
                        ins.then_inc(hot_ready, 1)

            def tile(s, g, j, par, stored=False):
                if s == 0:
                    if j == 0:
                        ve.wait_ge(g_in[par], g * 64 + (64 if par else 128))
                    other = gi[:, par, j, :]
                else:
                    other = gel[:, j % 4, :]
                if stored:
                    ve.wait_ge(a_in[j % 4], g * 32 + 16 * (j // 4 + 1))
                S.done(v_.tensor_tensor(gel[:, j % 4, :], gel[:, j % 4, :], other, ALU.mult))
                split_to(hid[par][0][:, j, :], hid[par][1][:, j, :], gel[:, j % 4, :]).then_inc(hid_ready[s], 1)

            def up(s, q, g, par):
                for j in range(8):
                    evacuated(q, j)
                    tile(s, g, j, par)

            def down(s, q):
                for j in range(8):
                    residual(q, j, 40 if s == 0 else None)

            def hidden(s, q8, groups):
                up(s, q8, 0, 0)
                with S.loop(groups // 2 - 1, 32) as i:
                    up(s, i * 4 + (q8 + 1), i * 2 + 1, 1)
                    down(s, i * 4 + (q8 + 2))
                    up(s, i * 4 + (q8 + 3), i * 2 + 2, 0)
                    down(s, i * 4 + (q8 + 4))
                e = q8 + 2 * groups - 3
                up(s, e, groups - 1, 1)
                down(s, e + 1)
                down(s, e + 2)

            def early_down(q, g, par):
                for j in range(8):
                    tile(0, g + 1, j, 1 - par, stored=True)
                    residual(q, j, 40)

            for j in range(8):
                tile(0, 0, j, 0, stored=True)
            q = Q_PEER + EARLY
            early_down(q, 0, 0)
            with S.loop(EARLY // 2 - 1, 32) as i:
                early_down(i * 2 + (q + 1), i * 2 + 1, 1)
                early_down(i * 2 + (q + 2), i * 2 + 2, 0)
            q += EARLY - 1
            with S.loop((16 - EARLY) // 2, 32) as i:
                up(0, i * 4 + q, i * 2 + EARLY, 0)
                down(0, i * 4 + (q + 1))
                up(0, i * 4 + (q + 2), i * 2 + (EARLY + 1), 1)
                down(0, i * 4 + (q + 3))
            down(0, Q_PEER + 31)
            norm(2, lambda k: col("final", k))

            def attention(s, r):
                a = att[s]
                norm(r, lambda k: col("mix0" if s == 0 else "mix1", k))

                def units(n, par, hh):
                    if isinstance(n, int):
                        ve.wait_ge(strip_in[s][hh], 16 * (n + 1))
                    else:
                        ve.wait_ge(strip_in[s][hh], n * 16 + 16)
                    for qt in range(TT):
                        ve.wait_ge(a["lg_done"], n * 8 + (4 * hh + qt + 1))
                        carry_waits()
                        S.done(v_.tensor_tensor_reduce(out=pb[:, par, hh, qt, :], in0=ps[:, qt, :],
                                                       in1=strip[:, hh, P * (3 - qt):P * (3 - qt) + T], scale=1.0, scalar=LOWEST,
                                                       op0=ALU.add, op1=ALU.max, accum_out=mx[:, hh, qt:qt + 1]))
                        v_.tensor_scalar(nm[:, hh, qt:qt + 1], mx[:, hh, qt:qt + 1], -1.0, None, ALU.mult).then_inc(a["nm_ready"], 1)

                def scale_a(n, par, hh):
                    for qt in range(TT):
                        ve.wait_ge(a["p_ready"], n * 8 + (4 * hh + qt + 1))
                        S.done(v_.reciprocal(rz[:, hh, qt:qt + 1], zt[:, hh, qt:qt + 1]))
                        v_.tensor_scalar(pb[:, par, hh, qt, :], pb[:, par, hh, qt, :], rz[:, hh, qt:qt + 1], None,
                                         ALU.mult).then_inc(a["pn_ready"], 1)
                    h = n * 2 + hh
                    sl = slice(h, h + 1) if isinstance(h, int) else bass.ds(h, 1)
                    v_.tensor_copy(zs[:, 0, sl, :], mx[:, hh, :].unsqueeze(1))
                    S.mark(v_.tensor_copy(zs[:, 1, sl, :], zt[:, hh, :].unsqueeze(1)))

                def combine_b(n, par):
                    for qt in range(TT):
                        ve.wait_ge(a["p_ready"], n * 8 + (4 + qt + 1))
                        S.mark(v_.reciprocal(rz[:, 0, qt:qt + 1], zt[:, 0, qt:qt + 1]))
                        S.done(v_.reciprocal(rz[:, 1, qt:qt + 1], zt[:, 1, qt:qt + 1]))
                        S.mark(v_.tensor_scalar(pb[:, par, 0, qt, :], pb[:, par, 0, qt, :], rz[:, 0, qt:qt + 1], None, ALU.mult))
                        S.done(v_.tensor_scalar(rz[:, 1, qt:qt + 1], rz[:, 1, qt:qt + 1], lamc[:, 3:4], None, ALU.mult))
                        v_.scalar_tensor_tensor(out=pb[:, par, 0, qt, :], in0=pb[:, par, 1, qt, :], scalar=rz[:, 1, qt:qt + 1],
                                                in1=pb[:, par, 0, qt, :], op0=ALU.mult, op1=ALU.add).then_inc(a["pn_ready"], 1)

                def out_b(u, par):
                    rsqrt(u + RS_B, P, 7)
                    S.done(v_.scalar_tensor_tensor(out=rt[:], in0=sq[:, 1 + par, :], scalar=subc[:, 0:1], in1=rstd[:],
                                                   op0=ALU.mult, op1=ALU.mult))
                    sl = slice(u, u + 1) if isinstance(u, int) else bass.ds(u, 1)
                    split_to(uT_r[:, sl, :], qT_r[:, sl, :], rt.unsqueeze(1)).then_inc(a["oT_ready"], 1)

                if s == 0:
                    with S.loop(4, 4 * 9) as i:
                        for par in range(2):
                            for hh in range(2):
                                units(i * 2 + par, par, hh)
                                scale_a(i * 2 + par, par, hh)
                    S.wait()
                    ve.sem_inc(a["lse"], 1)
                    ve.wait_ge(a["lse"], 2)
                    S.done(v_.tensor_tensor(zs[:, 0], zs[:, 0], zs[:, 2], ALU.add))
                    S.done(v_.tensor_reduce(gm[:, 0, :], zs[:, 0].rearrange("p h q -> p q h"), AX.X, ALU.max))
                    v_.tensor_tensor(zs[:, 0], zs[:, 0], gm[:, 0, :].unsqueeze(1).broadcast_to([P, A_HEADS, TT]), ALU.subtract).then_inc(a["lse"], 1)
                    ve.wait_ge(a["lse"], 4)
                    h0 = 0
                    for g, (_, _, nh) in enumerate(A_GROUPS):
                        S.done(v_.tensor_reduce(wg[:, g, :], zs[:, 1, h0:h0 + nh, :].rearrange("p h q -> p q h"), AX.X, ALU.add))
                        S.done(v_.tensor_scalar(wg[:, g, :], wg[:, g, :], 1.0 / nh, None, ALU.mult))
                        h0 += nh
                    S.done(v_.tensor_tensor(gm[:, 1, :], wg[:, 0, :], wg[:, 1, :], ALU.add))
                    S.done(v_.tensor_tensor(gm[:, 1, :], gm[:, 1, :], wg[:, 2, :], ALU.add))
                    S.done(v_.reciprocal(gm[:, 2, :], gm[:, 1, :]))
                    S.done(v_.tensor_scalar(gm[:, 2, :], gm[:, 2, :], float(len(A_GROUPS)), None, ALU.mult))
                    v_.tensor_tensor(wg[:], wg[:], gm[:, 2, :].unsqueeze(1).broadcast_to([P, 3, TT]), ALU.mult).then_inc(al_ready, 1)
                    ve.wait_ge(alb_sb, 3)
                    ve.wait_ge(a["o_ready"], 18)
                    h = 0
                    for g, (_, _, nh) in enumerate(A_GROUPS):
                        for _ in range(nh):
                            rows = slice(64 * (h % 2), 64 * (h % 2) + 64)
                            S.done(v_.tensor_tensor(qT[rows, h // 2, :], qT[rows, h // 2, :], alb[rows, g, :], ALU.mult))
                            if h % 2:
                                split_to(uT_r[:, h // 2, :], qT_r[:, h // 2, :], qT[:, h // 2, :]).then_inc(a["oT_ready"], 1)
                            h += 1
                else:
                    units(0, 0, 0)
                    units(0, 0, 1)
                    combine_b(0, 0)
                    with S.loop(3, 62) as i:
                        units(i * 2 + 1, 1, 0)
                        units(i * 2 + 1, 1, 1)
                        combine_b(i * 2 + 1, 1)
                        out_b(i * 2, 0)
                        units(i * 2 + 2, 0, 0)
                        units(i * 2 + 2, 0, 1)
                        combine_b(i * 2 + 2, 0)
                        out_b(i * 2 + 1, 1)
                    units(7, 1, 0)
                    units(7, 1, 1)
                    combine_b(7, 1)
                    out_b(6, 0)
                    out_b(7, 1)

            attention(0, 3)
            for j in range(KT):
                residual(Q_WO_A, j)
            norm(4, lambda k: col("mlp0", k))
            hidden(1, Q_MLP_A, 4)
            ve.wait_ge(lb_sem, 4)
            S.done(v_.tensor_tensor(lamc[:, 2:3], lamc[:, 1:2], lamc[:, 0:1], ALU.subtract))
            S.done(v_.tensor_scalar(lamc[:, 3:4], lamc[:, 2:3], -LAMBDA_INIT, None, ALU.add))
            attention(1, 5)
            for j in range(KT):
                residual(Q_WO_B, j)
            norm(6, lambda k: col("mlp1", k))
            hidden(2, Q_MLP_B, 4)
            norm(7, lambda k: col("final2", k))

        @block.gpsimd
        def _(po):
            for s in (v_free, og_ready, gmm_done, g_evac, att[0]["pt_ready"], att[1]["pt_ready"], att[0]["o_ready"]):
                po.sem_inc(s, 2)
            for s in (f_ready, lvl_evac, o_copied, att[1]["o_ready"]):
                po.sem_inc(s, 1)
            for s in (g_out, a_out):
                po.sem_inc(s, 16)

            with po.Fori(0, N_SPLIT // RING) as i:
                for j in range(RING):
                    po.wait_ge(hi_ready, i * RING + (j + 1))
                    g_.tensor_tensor(ring_r[:, j], ring[:, j], high_w[:, j], ALU.subtract).then_inc(lo_ready, 1)


def lay_out(inputs):
    f = {k: np.asarray(v) for k, v in inputs.items()}

    def pan(w):
        K, N = w.shape
        return w.reshape(K // D, KT, P, N // P, P).transpose(0, 3, 2, 1, 4)

    def hidden(up, down, groups):
        up = up.reshape(groups, 8, P, KT, P)
        out = [up[0]]
        for g in range(groups):
            if g + 1 < groups:
                out.append(up[g + 1])
            out.append(down[g])
        return out

    ada = pan(f["ada_w"][0])[0]
    z = pan(f["w_in"][0])[0].reshape(8, 8, P, KT, P)
    zq, zf, zi, zg, zca, zcb, zga, zgb = z
    seq = [ada[0:16]]
    seq.append(np.stack([zf, zq, zi, zg], 1).reshape(32, P, KT, P))
    rest = ada[16:48].reshape(8, 4, P, KT, P)
    seq.append(np.stack([zcb, zca, rest[:, 0], zga, rest[:, 1], zgb, rest[:, 2], rest[:, 3]], 1).reshape(64, P, KT, P))
    seq += [pan(f["w_a"][0])[0], pan(f["w_b"][0])[0], pan(f["w_out"][0])[0], pan(f["peer_wq"][0])[0]]
    up = f["peer_u"][0].reshape(NKEYS, P, KT, P).transpose(0, 3, 2, 1)
    up, down = (w.reshape(16, 8, P, KT, P) for w in (up, pan(f["peer_v"][0])))
    seq += [*up[:EARLY], *down[:EARLY - 1]]
    for g in range(EARLY, 16):
        seq += [up[g], down[g - 1]]
    seq.append(down[15])
    for s, (qkv, wo) in enumerate((("a_w_qkv_2", "a_w_o_2"), ("b_w_qkv_2", "b_w_o_2"))):
        seq += [pan(f[qkv][0])[0], pan(f[wo][0])[0]]
        seq += hidden(pan(f["mlp_w_in_2"][s])[0], pan(f["mlp_w_out_2"][s]), 4)
    panels = np.concatenate(seq, 0)
    assert panels.shape[0] == 8 * Q_END

    def c(a):
        return np.asarray(a).reshape(-1, P).T

    conv = f["conv_w"][0].reshape(CONV_K, KT, P).transpose(2, 1, 0).reshape(P, KT * CONV_K)
    cols = np.concatenate([
        c(f["c"]), c(f["ada_b"]), c(f["norm1_g"]), c(f["lb_logits"][0]), c(f["lb_logits"][1]), c(f["hg_norm_g"]), conv,
        c(f["conv_b"]), c(f["conv_ln_g"]), c(f["conv_ln_b"]), c(f["norm2_g"]), c(f["final_g"]),
        c(f["norm_mix_g_2"][0]), c(f["norm_mix_g_2"][1]), c(f["norm_mlp_g_2"][0]), c(f["norm_mlp_g_2"][1]),
        c(f["norm_final_g_2"]), c(f["b_subln_g_2"])], 1)
    consts = np.concatenate([np.eye(P, dtype=np.float32), np.tile(np.arange(P, dtype=np.float32), (P, 1))], 1)
    s_, t_ = np.arange(P)[:, None], np.arange(P)[None, :]
    masks = [((s_ // (2 * L) == t_ // (2 * L)) & (s_ % (2 * L) < L) & (t_ % (2 * L) >= L)) for L in LEVELS] + [s_ == t_]
    lmask = np.stack(masks, 1).astype(np.uint32)
    keysT = f["peer_keys"][0].reshape(16, NKEYS, P).transpose(2, 0, 1)
    rel = np.arange(1024) - 511
    n = np.abs(rel)
    nf = np.maximum(n, 1).astype(np.float32)
    large = 8 + (np.log(nf / np.float32(8)) / np.float32(np.log(1024 / 8)) * np.float32(8)).astype(np.int32)
    bucket = np.where(rel > 0, 16, 0) + np.where(n < 8, n, np.minimum(large, 15))
    oh = np.zeros((35, 2, 1024), np.float32)
    oh[:32] = (bucket[None, :] == np.arange(32)[:, None])[:, None, :]
    member = np.zeros((3, A_HEADS), np.float32)
    h0 = 0
    for g, (win, dil, nh) in enumerate(A_GROUPS):
        side = win // (2 * dil)
        oh[32 + g, 0] = np.where((n <= side * dil) & (n % dil == 0), 0.0, NEG)
        member[g, h0:h0 + nh] = 1.0
        h0 += nh
    return {
        "panels": panels, "xT": f["x"][0].T.reshape(KT, P, T).transpose(1, 0, 2), "cols": cols, "consts": consts,
        "lmask": lmask, "keysT": keysT, "oh": oh, "rel": np.concatenate([f["rel_bias_2"], member], 0),
        "blam": np.broadcast_to(f["b_lambda_2"].reshape(1, 4, 64), (P, 4, 64)),
    }


def kernel(**inputs):
    import concourse.bacc as bacc
    from concourse.bass_utils import run_bass_kernel_spmd

    nc = bacc.Bacc("TRN2", target_bir_lowering=False, num_devices=1)
    arrays, args = {}, []
    for name, a in lay_out(inputs).items():
        arrays[name] = np.ascontiguousarray(a)
        args.append(nc.dram_tensor(name, a.shape, mybir.dt.from_np(a.dtype), kind="ExternalInput").ap())
    F32 = mybir.dt.float32
    outT = nc.dram_tensor("outT", [P, KT, T], F32, kind="ExternalOutput").ap()
    gdram = nc.dram_tensor("gdram", [TT, NKEYS, P, P], F32, kind="Internal").ap()
    btab = nc.dram_tensor("btab", [2, A_HEADS, 1024], F32, kind="Internal").ap()
    strips_dram = nc.dram_tensor("strips_dram", [2 * A_HEADS, P, STRIP], F32, kind="Internal").ap()
    adram = nc.dram_tensor("adram", [8 * EARLY, P, T], F32, kind="Internal").ap()
    build(nc, *args, outT, gdram, adram, btab, strips_dram)
    r = run_bass_kernel_spmd(nc, [arrays], core_ids=[0])
    y = r.results[0]["outT"]
    return np.ascontiguousarray(np.asarray(y).transpose(2, 1, 0).reshape(1, T, D))
```
